# Optimizing a Trainium2 kernel written in Bass

```python
import math
import jax, jax.numpy as jnp
from jax import lax
import numpy as np

D_MODEL = 1024
BATCH = 1
SEQ = 256
DEPTH = 2

N_MIXERS = 3
PLE_DIM = 256
ROPE_THETA = 10000.0
NORM_EPS = 1e-6
POS_OFFSET_MAX = 4096

RET_HEADS = 4
RET_DK = D_MODEL // RET_HEADS
RET_DV = 2 * RET_DK
RET_CHUNK = 128

NSA_HEADS = 8
NSA_GROUPS = 2
NSA_DH = D_MODEL // NSA_HEADS
NSA_CMP_LEN = 32
NSA_CMP_STRIDE = 16
NSA_SEL_LEN = 64
NSA_TOP_N = 16
NSA_WINDOW = 512
NSA_CMP_HID = 256
NSA_SEL_Q_BLOCK = 16
NSA_WIN_Q_BLOCK = 128

S5_GROUP = 16
S5_GROUPS = D_MODEL // S5_GROUP
S5_STATE = 64

D_FF = 2816
N_EXPERTS = 8
TOP_K = 2
D_FF_EXPERT = 3584

kernel_name = "hybrid_retention_nsa_s5_moe_trunk"

def rms_norm(x, g):
    xf = x.astype(jnp.float32)
    y = xf * lax.rsqrt(jnp.mean(xf * xf, axis=-1, keepdims=True) + NORM_EPS)
    return (y * g.astype(jnp.float32)).astype(x.dtype)

def rope(x, pos):
    d = x.shape[-1]
    inv = ROPE_THETA ** (-jnp.arange(0, d, 2, dtype=jnp.float32) / d)
    ang = pos.astype(jnp.float32)[..., None] * inv
    cos = jnp.cos(ang)[..., None, :]
    sin = jnp.sin(ang)[..., None, :]
    xf = x.astype(jnp.float32)
    x1, x2 = xf[..., : d // 2], xf[..., d // 2:]
    return jnp.concatenate([x1 * cos - x2 * sin, x2 * cos + x1 * sin], axis=-1).astype(x.dtype)

def swiglu(h, w_gate_up, w_down):
    g, u = jnp.split(h @ w_gate_up, 2, axis=-1)
    return (jax.nn.silu(g) * u) @ w_down

def retention_mixer(xn, pos, w_in, gn, w_out):
    B, S, _ = xn.shape
    H, dk, dv, C = RET_HEADS, RET_DK, RET_DV, RET_CHUNK
    N = S // C
    q, k, v, g = jnp.split(xn @ w_in, [H * dk, 2 * H * dk, 2 * H * dk + H * dv], axis=-1)
    q = rope(q.reshape(B, S, H, dk), pos)
    k = rope(k.reshape(B, S, H, dk), pos) * (dk ** -0.5)
    v = v.reshape(B, S, H, dv)
    log_gamma = jnp.log1p(-jnp.exp2(-5.0 - jnp.arange(H, dtype=jnp.float32)))
    idx = jnp.arange(C, dtype=jnp.float32)
    diff = idx[:, None] - idx[None, :]
    d_mask = jnp.where(diff >= 0, jnp.exp(jnp.maximum(diff, 0.0) * log_gamma[:, None, None]), 0.0)
    q_decay = jnp.exp((idx + 1.0) * log_gamma[:, None])
    k_decay = jnp.exp((C - 1.0 - idx) * log_gamma[:, None])
    chunk_decay = jnp.exp(C * log_gamma)

    def chunks(t):
        return t.reshape(B, N, C, H, t.shape[-1]).transpose(1, 0, 3, 2, 4)

    def step(R, inp):
        qn, kn, vn = inp
        scores = jnp.einsum('bhid,bhjd->bhij', qn, kn) * d_mask
        intra = jnp.einsum('bhij,bhjv->bhiv', scores, vn)
        cross = jnp.einsum('bhid,bhdv->bhiv', qn, R) * q_decay[None, :, :, None]
        R_new = R * chunk_decay[None, :, None, None] + jnp.einsum(
            'bhjd,bhjv->bhdv', kn * k_decay[None, :, :, None], vn)
        return R_new, intra + cross

    R0 = jnp.zeros((B, H, dk, dv), jnp.float32)
    _, o = lax.scan(step, R0, (chunks(q), chunks(k), chunks(v)))
    o = o.transpose(1, 0, 3, 2, 4).reshape(B, S, H, dv)
    mu = jnp.mean(o, axis=-1, keepdims=True)
    var = jnp.mean(jnp.square(o - mu), axis=-1, keepdims=True)
    o = ((o - mu) * lax.rsqrt(var + NORM_EPS)).reshape(B, S, H * dv) * gn.astype(jnp.float32)
    return (o.astype(xn.dtype) * jax.nn.silu(g)) @ w_out

def nsa_mixer(xn, pos, w_in, q_norm, k_norm, cmp_pos, cmp_w1, cmp_w2, w_out):
    B, S, _ = xn.shape
    H, G, dh = NSA_HEADS, NSA_GROUPS, NSA_DH
    hg = H // G
    L, STR, SEL, WIN = NSA_CMP_LEN, NSA_CMP_STRIDE, NSA_SEL_LEN, NSA_WINDOW
    neg = jnp.finfo(jnp.float32).min
    scale = dh ** -0.5
    kvw = G * dh
    cuts = [int(c) for c in np.cumsum([H * dh, kvw, kvw, kvw, kvw, kvw, kvw])]
    q, kc, vc, ks, vs, kw, vw, gate = jnp.split(xn @ w_in, cuts, axis=-1)

    q = rope(rms_norm(q.reshape(B, S, H, dh), q_norm), pos).reshape(B, S, G, hg, dh)
    ks = rope(rms_norm(ks.reshape(B, S, G, dh), k_norm[1]), pos)
    kw = rope(rms_norm(kw.reshape(B, S, G, dh), k_norm[2]), pos)
    vs = vs.reshape(B, S, G, dh)
    vw = vw.reshape(B, S, G, dh)
    t_idx = jnp.arange(S)

    n_c = (S - L) // STR + 1
    blk = np.arange(n_c)[:, None] * STR + np.arange(L)[None, :]
    cmp_start = blk[:, 0]

    def compress(t, pos_emb, w1, w2):
        tb = t.reshape(B, S, G, dh)[:, blk] + pos_emb[None, None, :, None, :]
        tb = tb.transpose(0, 1, 3, 2, 4).reshape(B, n_c, G, L * dh)
        return jax.nn.gelu(tb @ w1) @ w2

    kc = compress(kc, cmp_pos[0], cmp_w1[0], cmp_w2[0])
    vc = compress(vc, cmp_pos[1], cmp_w1[1], cmp_w2[1])
    kc = rope(rms_norm(kc, k_norm[0]), pos[:, cmp_start])
    s_c = jnp.einsum('bsghd,bcgd->bghsc', q, kc).astype(jnp.float32) * scale
    valid_c = jnp.asarray(blk[:, -1])[None, :] <= t_idx[:, None]
    p_c = jax.nn.softmax(jnp.where(valid_c, s_c, neg), axis=-1)
    p_c = jnp.where(valid_c, p_c, 0.0)
    o_c = jnp.einsum('bghsc,bcgd->bsghd', p_c.astype(vc.dtype), vc)

    n_sel = S // SEL
    js = np.arange(n_sel)[None, :] * SEL
    cs = cmp_start[:, None]
    overlap = np.clip(np.minimum(cs + L, js + SEL) - np.maximum(cs, js), 0, None) / L
    M = jnp.asarray(overlap, dtype=jnp.float32)
    imp = jnp.einsum('bghsc,cj->bgsj', p_c, M)
    cur = (t_idx // SEL)[:, None]
    jb = jnp.arange(n_sel)[None, :]
    forced = (jb == 0) | (jb == cur) | (jb == cur - 1)
    imp = jnp.where(forced, jnp.inf, jnp.where(jb > cur, -jnp.inf, imp))
    _, sel_idx = lax.top_k(imp, min(NSA_TOP_N, n_sel))

    ks_b = ks.reshape(B, n_sel, SEL, G, dh).transpose(0, 3, 1, 2, 4)
    vs_b = vs.reshape(B, n_sel, SEL, G, dh).transpose(0, 3, 1, 2, 4)
    gather_blocks = jax.vmap(jax.vmap(lambda blocks, ix: blocks[ix]))

    QS = NSA_SEL_Q_BLOCK

    def sel_block(qb):
        q0 = qb * QS
        qblk = lax.dynamic_slice_in_dim(q, q0, QS, axis=1)
        ix = lax.dynamic_slice_in_dim(sel_idx, q0, QS, axis=2)
        t = q0 + jnp.arange(QS)
        k_sel = gather_blocks(ks_b, ix)
        v_sel = gather_blocks(vs_b, ix)
        s = jnp.einsum('btghd,bgtnkd->bghtnk', qblk, k_sel).astype(jnp.float32) * scale
        kpos = ix[..., None] * SEL + jnp.arange(SEL)
        mask = (kpos <= t[None, None, :, None, None])[:, :, None]
        s = jnp.where(mask, s, neg)
        sh = s.shape
        pr = jax.nn.softmax(s.reshape(sh[:4] + (-1,)), axis=-1).reshape(sh)
        return jnp.einsum('bghtnk,bgtnkd->btghd', pr.astype(v_sel.dtype), v_sel)

    o_s = lax.map(sel_block, jnp.arange(S // QS))
    o_s = o_s.transpose(1, 0, 2, 3, 4, 5).reshape(B, S, H, dh)

    QW = NSA_WIN_Q_BLOCK
    kw_p = jnp.pad(kw, ((0, 0), (WIN, 0), (0, 0), (0, 0)))
    vw_p = jnp.pad(vw, ((0, 0), (WIN, 0), (0, 0), (0, 0)))

    def win_block(qb):
        q0 = qb * QW
        qblk = lax.dynamic_slice_in_dim(q, q0, QW, axis=1)
        kwin = lax.dynamic_slice_in_dim(kw_p, q0, QW + WIN, axis=1)
        vwin = lax.dynamic_slice_in_dim(vw_p, q0, QW + WIN, axis=1)
        t = q0 + jnp.arange(QW)
        kpos = q0 - WIN + jnp.arange(QW + WIN)
        dist = t[:, None] - kpos[None, :]
        mask = (dist >= 0) & (dist < WIN) & (kpos >= 0)[None, :]
        s = jnp.einsum('btghd,bkgd->bghtk', qblk, kwin).astype(jnp.float32) * scale
        pr = jax.nn.softmax(jnp.where(mask, s, neg), axis=-1)
        return jnp.einsum('bghtk,bkgd->btghd', pr.astype(vwin.dtype), vwin)

    o_w = lax.map(win_block, jnp.arange(S // QW))
    o_w = o_w.transpose(1, 0, 2, 3, 4, 5).reshape(B, S, H, dh)

    gts = jax.nn.sigmoid(gate.reshape(B, S, H, 3))
    o = (gts[..., 0:1] * o_c.reshape(B, S, H, dh) + gts[..., 1:2] * o_s + gts[..., 2:3] * o_w)
    return o.reshape(B, S, H * dh) @ w_out

def s5_mixer(xn, w_in, a_re, a_im, b_re, b_im, c_re, c_im, d_skip, log_dt, w_glu):
    B, S, D = xn.shape
    G, P, Cg = S5_GROUPS, S5_STATE, S5_GROUP
    u = (xn @ w_in).astype(jnp.float32)
    ug = u.reshape(B, S, G, Cg)
    dt = jnp.exp(log_dt.astype(jnp.float32))[:, None]
    ar, ai = a_re.astype(jnp.float32), a_im.astype(jnp.float32)
    mag = jnp.exp(dt * ar)
    abar_re, abar_im = mag * jnp.cos(dt * ai), mag * jnp.sin(dt * ai)
    den = ar * ar + ai * ai
    nr, ni = abar_re - 1.0, abar_im
    f_re = (nr * ar + ni * ai) / den
    f_im = (ni * ar - nr * ai) / den
    br, bi = b_re.astype(jnp.float32), b_im.astype(jnp.float32)
    bbar_re = f_re[..., None] * br - f_im[..., None] * bi
    bbar_im = f_re[..., None] * bi + f_im[..., None] * br
    bu_re = jnp.einsum('bsgc,gpc->sbgp', ug, bbar_re)
    bu_im = jnp.einsum('bsgc,gpc->sbgp', ug, bbar_im)
    la_re = jnp.broadcast_to(abar_re[None, None], (S, 1, G, P))
    la_im = jnp.broadcast_to(abar_im[None, None], (S, 1, G, P))

    def combine(e1, e2):
        a1r, a1i, b1r, b1i = e1
        a2r, a2i, b2r, b2i = e2
        return (a2r * a1r - a2i * a1i, a2r * a1i + a2i * a1r,
                a2r * b1r - a2i * b1i + b2r, a2r * b1i + a2i * b1r + b2i)

    _, _, xr, xi = lax.associative_scan(combine, (la_re, la_im, bu_re, bu_im), axis=0)
    y = (jnp.einsum('sbgp,gcp->bsgc', xr, c_re.astype(jnp.float32))
         - jnp.einsum('sbgp,gcp->bsgc', xi, c_im.astype(jnp.float32)))
    y = y.reshape(B, S, D) + d_skip.astype(jnp.float32) * u
    y = jax.nn.gelu(y).astype(xn.dtype)
    a, b = jnp.split(y @ w_glu, 2, axis=-1)
    return a * jax.nn.sigmoid(b)

def moe_ffn(hn, router, w_gate_up, w_down):
    logits = (hn @ router).astype(jnp.float32)
    top_v, top_i = lax.top_k(logits, TOP_K)
    w = jax.nn.softmax(top_v, axis=-1)
    gates = jnp.sum(jax.nn.one_hot(top_i, N_EXPERTS, dtype=jnp.float32) * w[..., None], axis=-2)
    gates = gates.astype(hn.dtype)
    out = jnp.zeros_like(hn)
    for e in range(N_EXPERTS):
        out = out + gates[..., e:e + 1] * swiglu(hn, w_gate_up[e], w_down[e])
    return out

def setup_inputs(seed: int = 0) -> dict:
    key = jax.random.key(seed)
    keys = iter(jax.random.split(key, 64))
    f32 = jnp.float32
    D = D_MODEL

    def nrm(shape, scale):
        return jax.random.normal(next(keys), shape, f32) * scale

    def gain(shape):
        return 1.0 + 0.05 * jax.random.normal(next(keys), shape, f32)

    n_ret = len(range(0, DEPTH, N_MIXERS))
    n_nsa = len(range(1, DEPTH, N_MIXERS))
    n_s5 = len(range(2, DEPTH, N_MIXERS))
    n_dense = len(range(0, DEPTH, 2))
    n_moe = len(range(1, DEPTH, 2))
    ret_in = 2 * RET_HEADS * RET_DK + 2 * RET_HEADS * RET_DV
    nsa_in = NSA_HEADS * NSA_DH + 6 * NSA_GROUPS * NSA_DH + 3 * NSA_HEADS

    x = nrm((BATCH, SEQ, D), 1.0)
    p = nrm((DEPTH, BATCH, SEQ, PLE_DIM), 1.0)
    positions = (jax.random.randint(next(keys), (BATCH, 1), 0, POS_OFFSET_MAX, jnp.int32)
                 + jnp.arange(SEQ, dtype=jnp.int32)[None, :])
    a_re = -0.5 + 0.01 * jax.random.normal(next(keys), (n_s5, S5_GROUPS, S5_STATE), f32)
    a_im = (jnp.pi * jnp.arange(S5_STATE, dtype=f32)[None, None, :]
            + 0.01 * jax.random.normal(next(keys), (n_s5, S5_GROUPS, S5_STATE), f32))
    return {
        "x": x, "p": p, "positions": positions,
        "norm_mix": gain((DEPTH, D)), "norm_ffn": gain((DEPTH, D)), "norm_ple": gain((DEPTH, D)),
        "ret_w_in": nrm((n_ret, D, ret_in), D ** -0.5),
        "ret_gn": gain((n_ret, RET_HEADS * RET_DV)),
        "ret_w_out": nrm((n_ret, RET_HEADS * RET_DV, D), (RET_HEADS * RET_DV) ** -0.5),
        "nsa_w_in": nrm((n_nsa, D, nsa_in), D ** -0.5),
        "nsa_q_norm": gain((n_nsa, NSA_DH)),
        "nsa_k_norm": gain((n_nsa, 3, NSA_DH)),
        "nsa_cmp_pos": nrm((n_nsa, 2, NSA_CMP_LEN, NSA_DH), 0.1),
        "nsa_cmp_w1": nrm((n_nsa, 2, NSA_CMP_LEN * NSA_DH, NSA_CMP_HID), (NSA_CMP_LEN * NSA_DH) ** -0.5),
        "nsa_cmp_w2": nrm((n_nsa, 2, NSA_CMP_HID, NSA_DH), NSA_CMP_HID ** -0.5),
        "nsa_w_out": nrm((n_nsa, NSA_HEADS * NSA_DH, D), (NSA_HEADS * NSA_DH) ** -0.5),
        "s5_w_in": nrm((n_s5, D, D), D ** -0.5),
        "s5_a_re": a_re, "s5_a_im": a_im,
        "s5_b_re": nrm((n_s5, S5_GROUPS, S5_STATE, S5_GROUP), (2 * S5_GROUP) ** -0.5),
        "s5_b_im": nrm((n_s5, S5_GROUPS, S5_STATE, S5_GROUP), (2 * S5_GROUP) ** -0.5),
        "s5_c_re": nrm((n_s5, S5_GROUPS, S5_GROUP, S5_STATE), (2 * S5_STATE) ** -0.5),
        "s5_c_im": nrm((n_s5, S5_GROUPS, S5_GROUP, S5_STATE), (2 * S5_STATE) ** -0.5),
        "s5_d": nrm((n_s5, D), 0.5),
        "s5_log_dt": jax.random.uniform(next(keys), (n_s5, S5_GROUPS), f32, math.log(1e-3), math.log(1e-1)),
        "s5_w_glu": nrm((n_s5, D, 2 * D), D ** -0.5),
        "ffn_w_gate_up": nrm((n_dense, D, 2 * D_FF), D ** -0.5),
        "ffn_w_down": nrm((n_dense, D_FF, D), D_FF ** -0.5),
        "moe_router": nrm((n_moe, D, N_EXPERTS), D ** -0.5),
        "moe_w_gate_up": nrm((n_moe, N_EXPERTS, D, 2 * D_FF_EXPERT), D ** -0.5),
        "moe_w_down": nrm((n_moe, N_EXPERTS, D_FF_EXPERT, D), D_FF_EXPERT ** -0.5),
        "ple_w_proj": nrm((DEPTH, PLE_DIM, D), PLE_DIM ** -0.5),
        "ple_w_gate": nrm((DEPTH, D, D), D ** -0.5),
    }

def reference(x, p, positions, norm_mix, norm_ffn, norm_ple,
              ret_w_in, ret_gn, ret_w_out,
              nsa_w_in, nsa_q_norm, nsa_k_norm, nsa_cmp_pos, nsa_cmp_w1, nsa_cmp_w2, nsa_w_out,
              s5_w_in, s5_a_re, s5_a_im, s5_b_re, s5_b_im, s5_c_re, s5_c_im, s5_d, s5_log_dt, s5_w_glu,
              ffn_w_gate_up, ffn_w_down,
              moe_router, moe_w_gate_up, moe_w_down,
              ple_w_proj, ple_w_gate):
    h = x
    for i in range(DEPTH):
        m, j = i % N_MIXERS, i // N_MIXERS
        hn = rms_norm(h, norm_mix[i])
        if m == 0:
            y = retention_mixer(hn, positions, ret_w_in[j], ret_gn[j], ret_w_out[j])
        elif m == 1:
            y = nsa_mixer(hn, positions, nsa_w_in[j], nsa_q_norm[j], nsa_k_norm[j], nsa_cmp_pos[j],
                          nsa_cmp_w1[j], nsa_cmp_w2[j], nsa_w_out[j])
        else:
            y = s5_mixer(hn, s5_w_in[j], s5_a_re[j], s5_a_im[j], s5_b_re[j], s5_b_im[j],
                         s5_c_re[j], s5_c_im[j], s5_d[j], s5_log_dt[j], s5_w_glu[j])
        h = h + y.astype(h.dtype)
        hn = rms_norm(h, norm_ffn[i])
        if i % 2 == 0:
            f = swiglu(hn, ffn_w_gate_up[i // 2], ffn_w_down[i // 2])
        else:
            f = moe_ffn(hn, moe_router[i // 2], moe_w_gate_up[i // 2], moe_w_down[i // 2])
        h = h + f.astype(h.dtype)
        gate = jax.nn.sigmoid(rms_norm(h, norm_ple[i]) @ ple_w_gate[i])
        h = h + (gate * (p[i] @ ple_w_proj[i])).astype(h.dtype)
    return h


_drawn_inputs = setup_inputs


def setup_inputs(seed=0):
    import zlib

    import numpy as np

    out = dict(_drawn_inputs(seed))
    spreads = {}
    factors = {'norm_ple': 2.883, 'nsa_q_norm': 8.0, 'nsa_k_norm': 5.341}
    for name, (base, spread) in spreads.items():
        noise = np.random.default_rng([zlib.crc32(name.encode()), seed]).standard_normal(out[name].shape)
        drawn = base * np.exp(spread * noise) if base else spread * noise
        out[name] = __import__('jax').numpy.asarray(drawn.astype(out[name].dtype))
    for name, factor in factors.items():
        out[name] = (out[name] * factor).astype(out[name].dtype)
    return out
```

```python
from contextlib import ExitStack

import numpy as np

import concourse.bass as bass
from concourse import mybir

F32 = mybir.dt.float32
F32R = mybir.dt.float32r
I32 = mybir.dt.int32
U32 = mybir.dt.uint32
ACT = mybir.ActivationFunctionType
ALU = mybir.AluOpType
AXX = mybir.AxisListType.X

P = 128
D = 1024
S = 256
NT = S // P
KT = D // P
EPS = 1e-6
SLAB = 2048
RH, RDK, RDV = 4, 256, 512
NH, NG, DH = 8, 2, 128
LC, STR = 32, 16
NCB = (S - LC) // STR + 1
NE = 8
FF, FE = 2816, 3584
FSTEPS, ESTEPS = FF // 256, FE // 256
NEG = -1e30
TWO_PI = 2 * np.pi

A_RIN, A_ROUT, A_FFN = 0, 24, 32
A_P0 = A_FFN + 3 * FSTEPS
A_NIN = A_P0 + 6
A_CMP = A_NIN + 10
A_NOUT = A_CMP + 8
A_END = A_NOUT + 4
ESLABS = 3 * ESTEPS
RA, RB, RW = 3, 7, 3
LEAD1, LEAD2 = 2, 4

C_ID, C_IOTA, C_TRI, C_ONES = 0, 128, 256, 384
C_DEC = 512
C_M384 = C_DEC + RH * 256
C_INV = C_M384 + 384
C_I8 = C_INV + 128
C_CADD = C_I8 + 8
C_C01 = C_CADD + NT * NCB
C_END = C_C01 + NT * NCB
W_GAIN = 0
W_REP = 64
W_POS = W_REP + 4 * DH
W_W2 = W_POS + 2 * LC
W_GR = W_W2 + 2 * 2 * DH
W_END = W_GR + KT * 32


def const_array():
    c = np.zeros((P, C_END), np.float32)
    i = np.arange(P)
    c[:, C_ID:C_ID + P] = np.eye(P)
    c[:, C_IOTA:C_IOTA + P] = i[None, :]
    c[:, C_TRI:C_TRI + P] = i[:, None] < i[None, :]
    c[:, C_ONES:C_ONES + P] = 1
    t = np.arange(S)
    diff = t[None, :] - i[:, None]
    for h in range(RH):
        lg = np.log1p(-np.exp2(-5.0 - h))
        c[:, C_DEC + h * 256:C_DEC + (h + 1) * 256] = np.where(
            diff >= 0, np.exp(np.maximum(diff, 0) * lg), 0) * RDK ** -0.5
    causal = np.where(i[:, None] >= i[None, :], 0, NEG)
    c[:, C_M384:C_M384 + P] = causal
    c[:, C_M384 + 2 * P:C_M384 + 3 * P] = causal
    d = 2 * P
    c[:, C_INV:C_INV + P] = (np.float32(10000.0) ** (-np.arange(0, d, 2, dtype=np.float32) / np.float32(d)))[None, :]
    c[:, C_I8:C_I8 + 8] = np.arange(8)[None, :]
    end = np.arange(NCB) * STR + LC - 1
    for tt in range(NT):
        ok = end[None, :] <= (tt * P + i)[:, None]
        c[:, C_CADD + tt * NCB:C_CADD + (tt + 1) * NCB] = np.where(ok, 0, NEG)
        c[:, C_C01 + tt * NCB:C_C01 + (tt + 1) * NCB] = ok
    return c


T_NORM0, T_QK, T_Z, T_NORM1, T_NORM2, T_NORM3 = 0, 4, 12, 20, 24, 28
T_KV = T_NORM3 + 4
T_HID = T_KV + 2
T_Q12 = T_HID + 1
T_KC = T_Q12 + 6
T_PC = T_KC + 1
T_P = T_PC + 4
T_NORM4 = T_P + 2 * NH
T_NORM5 = T_NORM4 + 4
T_END = T_NORM5 + 4
T_SPLIT = [True] * T_END
for _k in [*range(T_QK, T_Z), *range(T_KV, T_NORM4)]:
    T_SPLIT[_k] = False


def t_bank_of(k):
    for k0 in (T_NORM0, T_NORM1, T_NORM2, T_NORM3, T_NORM4, T_NORM5):
        if k0 <= k < k0 + 4:
            return 4 + k - k0
    return 4 + k % 2


def t_before(k):
    return next((j for j in range(k - 1, -1, -1) if t_bank_of(j) == t_bank_of(k)), None)


def lows(k):
    return sum(T_SPLIT[:k + 1])


CH_RIN, CH_O, CH_ROUT, CH_FFN, CH_PROJ0, CH_GATE0, CH_NIN, CH_CMP = 0, 12, 16, 18, 20, 22, 24, 29
CH_NO = 31
CH_NOUT, CH_PROJ1, CH_GATE1 = 39, 41, 43


def build(nc, x, pos, consts, small, grep_in, w_static, w_expert, out):
    with ExitStack() as ctx:
        def sb(name, shape, dt=F32):
            return ctx.enter_context(nc.sbuf_tensor(name, shape, dt))

        def sem(name):
            return ctx.enter_context(nc.semaphore(name))

        WH = sb("weights_high", [P, RW, SLAB], F32R)
        WL = sb("weights_low", [P, RW, SLAB], F32R)
        RAWA = sb("raw_static", [P, RA, SLAB])
        BIG = sb("scratch", [P, 8 * SLAB])
        h = sb("residual", [P, NT, D])
        RT = sb("activations_t", [P, 4 * SLAB], F32R)
        AT = sb("hidden_t", [P, SLAB], F32R)
        C = sb("consts_sb", [P, C_END])
        W = sb("small_sb", [P, W_END])
        COS = sb("cos", [P, 3, P])
        SIN = sb("sin", [P, 3, P])
        GRH = sb("gate_router_high", [P, KT, 32], F32R)
        GRL = sb("gate_router_low", [P, KT, 32], F32R)
        ST = sb("scores_t", [P, 2, 384])
        Q = sb("stats", [P, 400])
        posi = sb("pos_int", [P, 4], I32)
        idx = sb("top_index", [P, NT, 8], U32)
        n_sb = sb("loop_counts", [P, 2], I32)
        PS = ctx.enter_context(nc.psum_tensor("banks", [P, 8, 512], F32))

        def cols(base, n):
            return C[:, base:base + n]

        ident = cols(C_ID, P)
        gain = lambda norm, kt: W[:, W_GAIN + norm * KT + kt:W_GAIN + norm * KT + kt + 1]
        rep = lambda i: W[:, W_REP + i * DH:W_REP + (i + 1) * DH]

        XTH = RT[:, 0:2048].rearrange("p (k t) -> p k t", k=KT)
        XTL = RT[:, 2048:4096].rearrange("p (k t) -> p k t", k=KT)
        ZTH = RT[:, 0:4096].rearrange("p (k t) -> p k t", k=16)
        ZTL = RT[:, 4096:8192].rearrange("p (k t) -> p k t", k=16)
        V = BIG[:, 0:4096].rearrange("p (t n) -> p t n", t=NT)
        SG = BIG[:, 4096:8192].rearrange("p (t n) -> p t n", t=NT)
        TC = BIG[:, 4096:4608]
        TS = BIG[:, 4608:5120]
        O = BIG[:, 8192:12288].rearrange("p (t n) -> p t n", t=NT)
        QKT = BIG[:, 12288:16384].rearrange("p (k t) -> p k t", k=16)
        XN = BIG[:, 14336:16384].rearrange("p (t n) -> p t n", t=NT)
        SIG = BIG[:, 14336:14848].rearrange("p (t n) -> p t n", t=NT)
        HID = BIG[:, 14848:15360].rearrange("p (t n) -> p t n", t=NT)
        GSEL = BIG[:, 15360:15616].rearrange("p (t n) -> p t n", t=NT)
        PP = BIG[:, 0:2048].rearrange("p (t n) -> p t n", t=NT)
        PG = BIG[:, 2048:4096].rearrange("p (t n) -> p t n", t=NT)
        Q12 = BIG[:, 0:3072].rearrange("p (t h d) -> p t h d", t=NT, h=12)
        TBR = BIG[:, 3072:4032]
        NC1 = BIG[:, 4096:7168].rearrange("p (t h d) -> p t h d", t=NT, h=12)
        VN = BIG[:, 7168:8192].rearrange("p (t b d) -> p t b d", t=NT, b=4)
        NC2 = BIG[:, 8192:11264].rearrange("p (t h d) -> p t h d", t=NT, h=12)
        GEL = BIG[:, 11264:12288].rearrange("p (i n) -> p i n", i=4)
        PCT = BIG[:, 8192:10240].rearrange("p (h t) -> p h t", h=NH)
        PT = BIG[:, 10240:11008].rearrange("p (b n) -> p b n", b=2)
        KVN = BIG[:, 12288:13312].rearrange("p (t b d) -> p t b d", t=NT, b=4)
        QT = BIG[:, 12288:15360].rearrange("p (h t) -> p h t", h=12)
        KVT = BIG[:, 15360:16384].rearrange("p (b t) -> p b t", b=4)
        CSC = BIG[:, 4096:4352].rearrange("p (m c) -> p m c", m=16)
        CV = BIG[:, 4608:5120].rearrange("p (b d) -> p b d", b=4)
        CSQ = BIG[:, 5120:5632].rearrange("p (b d) -> p b d", b=4)
        HT = BIG[:, 5632:5760].rearrange("p (b c) -> p b c", b=4)
        KCT = BIG[:, 5760:5792].rearrange("p (g c) -> p g c", g=NG)
        TBH = [RT[:, 4096 + i * 1920:4096 + i * 1920 + 960] for i in range(2)]
        TBL = [RT[:, 5056 + i * 1920:5056 + i * 1920 + 960] for i in range(2)]
        GREP = BIG[:, 12288:13312]
        XGH = RT[:, 0:1024].rearrange("p (k t) -> p k t", k=KT)
        XGL = RT[:, 1024:2048].rearrange("p (k t) -> p k t", k=KT)
        YH = RT[:, 2048:3072]
        YL = RT[:, 3072:4096]
        XNH = RT[:, 4096:6144].rearrange("p (t n) -> p t n", t=NT)
        XNL = RT[:, 6144:8192].rearrange("p (t n) -> p t n", t=NT)
        GTH = AT[:, 1024:1280]
        GTL = AT[:, 1280:1536]
        SEL = AT[:, 1536:1792].rearrange("p (t n) -> p t n", t=NT)

        ms, rt, rstd = (Q[:, 2 * i:2 * i + 2] for i in range(3))
        posf = Q[:, 8:11]
        ss = Q[:, 32:36]
        bst = Q[:, 12:24].rearrange("p (t n) -> p t n", t=NT)
        mv = Q[:, 24:28].rearrange("p (t n) -> p t n", t=NT)
        vr, vs_, vq = Q[:, 28:30], Q[:, 30:32], Q[:, 6:8]
        ssq, msq, rsq, riq = (Q[:, 36 + 24 * i:60 + 24 * i] for i in range(4))
        gates = Q[:, 132:180].rearrange("p (t n) -> p t n", t=NT)
        cmx, csm, crc = (Q[:, 180 + 16 * i:196 + 16 * i] for i in range(3))
        nmx = Q[:, 228:232].rearrange("p (b t) -> p b t", b=2)
        sme = Q[:, 232:236].rearrange("p (b t) -> p b t", b=2)
        rce = Q[:, 236:240].rearrange("p (b t) -> p b t", b=2)
        lg = Q[:, 240:256].rearrange("p (t e) -> p t e", t=NT)
        mx8 = Q[:, 256:272].rearrange("p (t e) -> p t e", t=NT)
        ixf = Q[:, 272:288].rearrange("p (t e) -> p t e", t=NT)
        dif, e2, w1, w2, den = (Q[:, 288 + 2 * i:290 + 2 * i] for i in range(5))
        oh1 = Q[:, 298:314].rearrange("p (t e) -> p t e", t=NT)
        oh2 = Q[:, 314:330].rearrange("p (t e) -> p t e", t=NT)
        RK = Q[:, 330:364].rearrange("p (t r) -> p t r", t=NT)
        GT2 = Q[:, 364:396].rearrange("p (t r) -> p t r", t=NT)
        mxc, nfl = Q[:, 396:397], Q[:, 397:399]

        x_in, pos_in, const_in, small_in, grep_ld, out_st = (
            sem(n) for n in ("x_in", "pos_in", "const_in", "small_in", "grep_in", "out_stored"))
        landA = [sem(f"static_slab_in{i}") for i in range(RA)]
        landB = [sem(f"expert_slab_in{i}") for i in range(RB)]
        high_ready, low_ready, slab_used = sem("high_ready"), sem("low_ready"), sem("slab_used")
        bank_free = sem("bank_free")
        t_done, t_high, t_low = sem("t_done"), sem("t_high"), sem("t_low")
        dve_step, hid_step = sem("dve_step"), sem("hid_step")
        sq_done, ms_done, rt_done, xn_done = sem("sq_done"), sem("ms_done"), sem("rt_done"), sem("xn_done")
        ang_done, trig_done, gr_high, gr_low = sem("ang_done"), sem("trig_done"), sem("gr_high"), sem("gr_low")
        rope_done, v_done, sig_done, sg_done = sem("rope_done"), sem("v_done"), sem("g_sigmoid"), sem("g_silu")
        sc_done, st_done, o_mm, o_copied = sem("ret_scores"), sem("ret_masked"), sem("ret_out_mm"), sem("ret_out_copied")
        var_done, std_done, z_done, zs_done = sem("ret_var"), sem("ret_std"), sem("ret_z"), sem("ret_z_scaled")
        h_ready = sem("residual_ready")
        f_sig, f_hid, f_t, f_high, f_low, f_acc = (
            sem(n) for n in ("ffn_sigmoid", "ffn_hidden", "ffn_hidden_t", "ffn_t_high", "ffn_t_low", "ffn_acc_read"))
        pp_done, pg_done = sem("ple_proj_copied"), sem("ple_gate_sigmoid")
        n_copied, n_sq, n_ms, n_rt, n_rope = (
            sem(n) for n in ("nsa_copied", "nsa_squares", "nsa_mean_squares", "nsa_root", "nsa_roped"))
        tb_raw, tb_high, tb_low = sem("blocks_raw"), sem("blocks_high"), sem("blocks_low")
        gate_mm, gate_sig = sem("gate_logits"), sem("gates_ready")
        g_sq, g_in, g_sg, g_hid = sem("gelu_square"), sem("gelu_inner"), sem("gelu_sigmoid"), sem("gelu_hidden")
        c2_mm, c2_cp, kc_sq, kc_ms, kc_rt, kc_rope = (
            sem(n) for n in ("cmp_kv_mm", "cmp_kv_copied", "kc_squares", "kc_mean", "kc_root", "kc_roped"))
        cs_mm, cs_sub, cs_exp, cp_done = sem("cmp_scores"), sem("cmp_shifted"), sem("cmp_exp"), sem("cmp_probs")
        as_mm, as_msk, as_exp, ap_done, av_mm, oh_done, ol_done = (
            sem(n) for n in ("att_scores", "att_masked", "att_exp", "att_probs", "att_values", "att_o_high", "att_o_low"))
        rl_mm, rl_d, rl_e, rl_mask, rk_mm, n_ready = (
            sem(n) for n in ("router_logits", "router_diff", "router_exp", "router_mask", "rank_mm", "counts_ready"))
        xg_f, xg_h, xg_l = sem("x_gained"), sem("x_nat_high"), sem("x_nat_low")
        e_sel, e_ga, e_xh, e_xl, e_gsel, e_gt, e_gth, e_gtl = (
            sem(n) for n in ("sel_ready", "gathered", "gather_high", "gather_low", "gate_sel_ready", "gate_t",
                             "gate_t_high", "gate_t_low"))
        e_yh, e_yl, e_sc, e_add = sem("y_high"), sem("y_low"), sem("scattered"), sem("expert_added")

        static = w_static
        block = ctx.enter_context(nc.Block())

        def tbank(k):
            return PS[:, t_bank_of(k), :]

        def pair(c, tt):
            return PS[:, 2 * (c % 2) + tt, :]

        def gu_slab(n):
            return 0 if n == 0 else 3 * n - 1

        def down_slab(n, steps):
            return 3 * n + 4 if n < steps - 1 else 3 * steps - 1

        @block.sync
        def _(sp):
            sp.dma_start(h[:, :, :], x.rearrange("(t p) d -> p t d", p=P)).then_inc(x_in, 16)
            sp.dma_start(posi[:, :], pos).then_inc(pos_in, 16)
            sp.dma_start(C[:, :], consts).then_inc(const_in, 16)
            sp.dma_start(W[:, :], small).then_inc(small_in, 16)

            def load(s, w=SLAB):
                if s >= RA:
                    sp.wait_ge(low_ready, s - RA + 1)
                sp.dma_start(RAWA[:, s % RA, 0:w], static[s, :, 0:w]).then_inc(landA[s % RA], 16)

            for s in range(A_END):
                load(s, 512 if s == A_P0 else SLAB)
            for s in range(A_END, A_END + RA):
                load(s, 512 if s == A_END else SLAB)
            sp.wait_ge(av_mm, 2 * NH)
            sp.dma_start(GREP, grep_in).then_inc(grep_ld, 16)

            def expert_slabs(e, b):
                for j in range(ESLABS):
                    sp.wait_ge(low_ready, b + (A_END + j - RB + 1))
                    if j == RB - 1:
                        sp.wait_ge(xg_f, 2)
                    sp.dma_start(BIG[:, (j % RB) * SLAB:(j % RB + 1) * SLAB],
                                 w_expert[bass.ds(e, 1), j, :, :].rearrange("o p n -> p (o n)")
                                 ).then_inc(landB[j % RB], 16)

            with sp.Fori(0, NE, 1) as e:
                expert_slabs(e, e * ESLABS)
            sp.wait_ge(n_ready, 1)
            rounds = sp.value_load(n_sb[0:1, 1:2], min_val=1, max_val=2)
            with sp.If(rounds > 1):
                with sp.Fori(0, NE, 1) as e:
                    expert_slabs(e, (e + NE) * ESLABS)
            done = rounds * (NE * ESLABS)
            for s in range(A_END + RA, A_END + 6):
                sp.wait_ge(low_ready, done + (s - RA + 1))
                sp.dma_start(RAWA[:, s % RA, :], static[s, :, :]).then_inc(landA[s % RA], 16)
            for c in range(2):
                sp.wait_ge(h_ready, 11 + c)
                sp.dma_start(out.rearrange("(t p) d -> p t d", p=P)[:, :, c * 512:(c + 1) * 512],
                             h[:, :, c * 512:(c + 1) * 512]).then_inc(out_st, 16)
            sp.wait_ge(out_st, 32)

        @block.tensor
        def _(pe):
            def three(outs, lhs, rhs, first, last):
                for o, (xh, xl) in zip(outs, lhs):
                    for oo, (wh, wl) in zip(o, rhs):
                        pe.matmul(oo, xh, wh, start=first, stop=False)
                        pe.matmul(oo, xh, wl, start=False, stop=False)
                        m = pe.matmul(oo, xl, wh, start=False, stop=last)
                return m

            def slab_mm(used, slot, kts, width, outs, lhs_of, first, last, k0=None):
                if k0 is not None:
                    pe.wait_ge(t_low, lows(k0 + kts[-1] // 2))
                pe.wait_ge(low_ready, used + 1)
                for i, kt in enumerate(kts):
                    rhs = []
                    n = len(outs[0])
                    for c in range(n):
                        a = i * width + c * (width // n)
                        rhs.append((WH[:, slot, a:a + width // n], WL[:, slot, a:a + width // n]))
                    m = three(outs, lhs_of(kt), rhs, first and i == 0, last and i == len(kts) - 1)
                m.then_inc(slab_used, 1)

            def xt(kt):
                return [(XTH[:, kt, tt * P:(tt + 1) * P], XTL[:, kt, tt * P:(tt + 1) * P]) for tt in range(NT)]

            def zt(kt):
                return [(ZTH[:, kt, tt * P:(tt + 1) * P], ZTL[:, kt, tt * P:(tt + 1) * P]) for tt in range(NT)]

            def chunk_free(c):
                if c >= 2:
                    pe.wait_ge(bank_free, c - 1)

            def chunk(c, s, lhs_of, nk=KT, k0=None):
                chunk_free(c)
                for i in range(nk // 4):
                    slab_mm(s + i, (s + i) % RW, range(4 * i, 4 * i + 4), 512,
                            [[pair(c, tt)] for tt in range(NT)], lhs_of, i == 0, i == nk // 4 - 1, k0)

            def t_free(k):
                j = t_before(k)
                if j is not None and T_SPLIT[j]:
                    pe.wait_ge(t_low, lows(j))
                elif j is not None:
                    pe.wait_ge(t_high, j + 1)

            def t_step(k, blocks):
                t_free(k)
                for o, b in blocks:
                    m = pe.transpose(o, b, ident)
                m.then_inc(t_done, 1)

            def norm_t(n, k0):
                pe.wait_ge(xn_done, 2 * (n + 1))
                for q in range(4):
                    b = tbank(k0 + q)
                    t_step(k0 + q, [(b[:, (i * NT + tt) * P:(i * NT + tt + 1) * P],
                                     XN[:, tt, (2 * q + i) * P:(2 * q + i + 1) * P])
                                    for i in range(2) for tt in range(NT)])

            def ffn(steps, base, lhs_of, tiles, gu_bank, t_bank, acc, fbase, after_gu=lambda n: None,
                    k0=None):
                def at(n, k):
                    w = tiles * P
                    a = (n % 2) * 4 * w + k * w
                    return [(AT[:, a + tt * P:a + (tt + 1) * P], AT[:, a + 2 * w + tt * P:a + 2 * w + (tt + 1) * P])
                            for tt in range(tiles)]

                def transposes(n):
                    pe.wait_ge(f_hid, fbase + (n + 1))
                    for i in range(2):
                        for tt in range(tiles):
                            m = pe.transpose(t_bank(n)[:, (i * tiles + tt) * P:(i * tiles + tt + 1) * P],
                                             HID[:, tt, i * P:(i + 1) * P], ident)
                    m.then_inc(f_t, 1)

                def down(n):
                    pe.wait_ge(f_low, fbase + (n + 1))
                    s = down_slab(n, steps)
                    slab_mm(base + s, s % RW if tiles == 1 else (base + s) % RW, range(2), D, acc,
                            lambda k: at(n, k), n == 0, n == steps - 1)

                for n in range(steps):
                    for i in range(2):
                        s = gu_slab(n) + i
                        if n >= tiles % 2 + 1 and i == 0:
                            pe.wait_ge(f_hid, fbase + (n - tiles % 2))
                        slab_mm(base + s, s % RW if tiles == 1 else (base + s) % RW, range(4 * i, 4 * i + 4), 512,
                                [[gu_bank(n, tt)] for tt in range(tiles)], lhs_of, i == 0, i == 1, k0 if n == 0 else None)
                        if i == 0 and n:
                            transposes(n - 1)
                    after_gu(n)
                    if n:
                        down(n - 1)
                transposes(steps - 1)
                down(steps - 1)

            def ple(c0, base, slot0, n, k0):
                chunk_free(c0)
                chunk_free(c0 + 1)
                sp_ = slot0 % RW
                pt = lambda k: [(WH[:, sp_, k * S + tt * P:k * S + (tt + 1) * P],
                                 WL[:, sp_, k * S + tt * P:k * S + (tt + 1) * P]) for tt in range(NT)]
                pe.wait_ge(low_ready, base + 2)
                for k in range(2):
                    rhs = [(WH[:, (slot0 + 1) % RW, k * D + c * 512:k * D + (c + 1) * 512],
                            WL[:, (slot0 + 1) % RW, k * D + c * 512:k * D + (c + 1) * 512]) for c in range(2)]
                    m = three([[pair(c0, tt), pair(c0 + 1, tt)] for tt in range(NT)], pt(k), rhs, k == 0, k == 1)
                m.then_inc(slab_used, 2)
                norm_t(n, k0)
                for c in range(2):
                    chunk_free(c0 + 2 + c)
                    for i in range(2):
                        s = 2 + 2 * c + i
                        slab_mm(base + s, (slot0 + s) % RW, range(4 * i, 4 * i + 4), 512,
                                [[pair(c0 + 2 + c, tt)] for tt in range(NT)], xt, i == 0, i == 1, k0 if c == 0 else None)

            pe.wait_ge(const_in, 16)
            norm_t(0, T_NORM0)
            for c in range(12):
                chunk(CH_RIN + c, A_RIN + 2 * c, xt, k0=T_NORM0 if c == 0 else None)
                if 4 <= c:
                    q = c - 4
                    if q == 0:
                        pe.wait_ge(rope_done, 8)
                    b = tbank(T_QK + q)
                    t_step(T_QK + q, [(b[:, (i * NT + tt) * P:(i * NT + tt + 1) * P],
                                       O[:, tt, (2 * q + i) * P:(2 * q + i + 1) * P])
                                      for i in range(2) for tt in range(NT)])
            pe.wait_ge(t_high, T_Z)
            pe.wait_ge(v_done, 8)

            def ret_scores(hd):
                if hd >= 2:
                    pe.wait_ge(st_done, hd - 1)
                b = PS[:, 6 + hd % 2, :]
                for jt, (o, i0) in enumerate((((0, 256), 0), ((256, 384), P))):
                    for k in range(2):
                        m = pe.matmul(b[:, o[0]:o[1]], QKT[:, 8 + 2 * hd + k, jt * P:(jt + 1) * P],
                                      QKT[:, 2 * hd + k, i0:S], start=k == 0, stop=k == 1)
                m.then_inc(sc_done, 1)

            def ret_values(hd):
                pe.wait_ge(st_done, hd + 1)
                c = CH_O + hd
                chunk_free(c)
                v = [V[:, tt, hd * RDV:(hd + 1) * RDV] for tt in range(NT)]
                s = ST[:, hd % 2, :]
                pe.matmul(pair(c, 0), s[:, 0:P], v[0], start=True, stop=True)
                pe.matmul(pair(c, 1), s[:, P:2 * P], v[0], start=True, stop=False)
                pe.matmul(pair(c, 1), s[:, 2 * P:3 * P], v[1], start=False, stop=True).then_inc(o_mm, 1)

            def z_t(hd):
                pe.wait_ge(zs_done, 2 * (hd + 1))
                for j in range(2):
                    k = T_Z + 2 * hd + j
                    f = 4 * hd + 2 * j
                    t_step(k, [(tbank(k)[:, (i * NT + tt) * P:(i * NT + tt + 1) * P],
                                O[:, tt, (f + i) * P:(f + i + 1) * P]) for i in range(2) for tt in range(NT)])

            ret_scores(0)
            for hd in range(RH):
                if hd + 1 < RH:
                    ret_scores(hd + 1)
                ret_values(hd)
                if hd:
                    z_t(hd - 1)
            z_t(RH - 1)
            pe.wait_ge(t_low, lows(T_NORM1 - 1))
            for c in range(2):
                chunk(CH_ROUT + c, A_ROUT + 4 * c, zt, 16)
            norm_t(1, T_NORM1)
            pe.wait_ge(bank_free, CH_FFN)
            pe.wait_ge(t_low, lows(T_NORM1 + 3))
            ffn(FSTEPS, A_FFN, xt, NT, lambda n, tt: PS[:, 6 + tt, :], lambda n: PS[:, 4 + n % 2, :],
                [[PS[:, tt, :], PS[:, 2 + tt, :]] for tt in range(NT)], 0, k0=T_NORM1)
            ple(CH_PROJ0, A_P0, A_P0, 2, T_NORM2)
            norm_t(3, T_NORM3)
            for c, cs in enumerate((2, 0, 1, 3, 4)):
                chunk(CH_NIN + c, A_NIN + 2 * c, xt, k0=T_NORM3 if c == 0 else None)
                if c == 1:
                    pe.wait_ge(n_copied, 2)
                    for q in range(2):
                        k = T_KV + q
                        t_step(k, [(tbank(k)[:, (i * NT + tt) * P:(i * NT + tt + 1) * P], KVN[:, tt, 2 * q + i, :])
                                   for i in range(2) for tt in range(NT)])
            pe.wait_ge(gr_low, 1)
            for tt in range(NT):
                for kt in range(KT):
                    m = three([[PS[:, 6, tt * 32:tt * 32 + 24]]], [xt(kt)[tt]],
                              [(GRH[:, kt, 0:24], GRL[:, kt, 0:24])], kt == 0, kt == KT - 1)
            m.then_inc(gate_mm, 1)
            pe.wait_ge(tb_low, 2)
            for kv in range(2):
                c = CH_CMP + kv
                chunk_free(c)
                for i in range(4):
                    slab_mm(A_CMP + 4 * kv + i, (A_CMP + 4 * kv + i) % RW, range(8 * i, 8 * i + 8), 256,
                            [[pair(c, 0)[:, 0:256]]],
                            lambda l: [(RT[:, 4096 + kv * 1920 + l * 30:4096 + kv * 1920 + l * 30 + P],
                                        RT[:, 5056 + kv * 1920 + l * 30:5056 + kv * 1920 + l * 30 + P])],
                            i == 0, i == 3)
            pe.wait_ge(g_hid, 2)
            b = tbank(T_HID)
            nb = NG * NCB
            t_free(T_HID)
            for i in range(4):
                m = pe.transpose(b[:, 32 * i:32 * i + nb], GEL[0:nb, 2 + i // 2, (i % 2) * P:(i % 2 + 1) * P],
                                 ident[0:nb, 0:nb])
            m.then_inc(t_done, 1)
            pe.wait_ge(t_high, T_HID + 1)
            for kv in range(2):
                for g in range(NG):
                    for k in range(2):
                        m = pe.matmul(PS[0:NCB, 7, (2 * kv + g) * DH:(2 * kv + g + 1) * DH],
                                      HT[:, 2 * kv + k, g * NCB:(g + 1) * NCB],
                                      W[:, W_W2 + (2 * kv + k) * DH:W_W2 + (2 * kv + k + 1) * DH],
                                      start=k == 0, stop=k == 1)
            m.then_inc(c2_mm, 1)
            pe.wait_ge(n_rope, 2)
            for q in range(6):
                k = T_Q12 + q
                t_step(k, [(tbank(k)[:, (i * NT + tt) * P:(i * NT + tt + 1) * P], Q12[:, tt, 2 * q + i, :])
                           for i in range(2) for tt in range(NT)])
            pe.wait_ge(kc_rope, 1)
            k = T_KC
            t_free(k)
            for g in range(NG):
                m = pe.transpose(tbank(k)[:, 16 * g:16 * g + NCB], CSQ[0:NCB, 2 + g, :], ident[0:NCB, 0:NCB])
            m.then_inc(t_done, 1)
            pe.wait_ge(t_high, k + 1)
            pe.wait_ge(gate_sig, 1)
            for tt in range(NT):
                for hd in range(NH):
                    m = pe.matmul(PS[:, 6, (tt * NH + hd) * 16:(tt * NH + hd) * 16 + NCB],
                                  QT[:, hd, tt * P:(tt + 1) * P], KCT[:, hd // 4, 0:NCB], start=True, stop=True)
            m.then_inc(cs_mm, 1)
            pe.wait_ge(cp_done, 1)
            for q in range(4):
                k = T_PC + q
                t_free(k)
                for i in range(2):
                    for tt in range(NT):
                        m = pe.matmul(tbank(k)[0:NCB, (i * NT + tt) * P:(i * NT + tt + 1) * P],
                                      CSC[:, tt * NH + 2 * q + i, 0:NCB], ident, start=True, stop=True)
                m.then_inc(t_done, 1)

            def att_scores(m_):
                hd, br = m_ // 2, m_ % 2
                if m_ >= 2:
                    pe.wait_ge(as_msk, m_ - 1)
                kk = 8 + 2 * br + hd // 4
                o = PS[:, 6 + m_ % 2, :]
                pe.matmul(o[:, 0:P], QT[:, hd, 0:P], QT[:, kk, 0:P], start=True, stop=True)
                pe.matmul(o[:, P:3 * P], QT[:, hd, P:S], QT[:, kk, :], start=True, stop=True).then_inc(as_mm, 1)

            def att_probs_t(m_):
                pe.wait_ge(ap_done, m_ + 1)
                k = T_P + m_
                t_step(k, [(tbank(k)[:, i * P:(i + 1) * P], ST[:, m_ % 2, i * P:(i + 1) * P]) for i in range(3)])

            def att_values(m_):
                hd, br = m_ // 2, m_ % 2
                c = CH_NO + hd
                o = pair(c, 0)
                if br == 0:
                    chunk_free(c)
                pe.wait_ge(t_high, T_P + m_ + 1)
                v = [VN[:, tt, 2 * br + hd // 4, :] for tt in range(NT)]
                pe.matmul(o[:, 0:S], v[0], PT[:, m_ % 2, 0:S], start=br == 0, stop=False)
                m = pe.matmul(o[:, P:S], v[1], PT[:, m_ % 2, S:S + P], start=False, stop=False)
                if br == 1:
                    m = pe.matmul(o[:, 0:S], CV[0:NCB, 2 + hd // 4, :], PCT[0:NCB, hd, :], start=False, stop=True)
                m.then_inc(av_mm, 1)

            pe.wait_ge(cs_sub, 1)
            pe.wait_ge(c2_cp, 1)
            att_scores(0)
            for i in range(2 * NH + 2):
                if i + 1 < 2 * NH:
                    att_scores(i + 1)
                if 1 <= i <= 2 * NH:
                    att_probs_t(i - 1)
                if i >= 2:
                    att_values(i - 2)
            pe.wait_ge(ol_done, NH)
            for c in range(2):
                chunk(CH_NOUT + c, A_NOUT + 2 * c, xt)
            norm_t(4, T_NORM4)
            pe.wait_ge(t_low, lows(T_NORM4 + 3))
            for tt in range(NT):
                for kt in range(KT):
                    m = three([[PS[:, 6, tt * 32:tt * 32 + 8]]], [xt(kt)[tt]],
                              [(GRH[:, kt, 24:32], GRL[:, kt, 24:32])], kt == 0, kt == KT - 1)
            m.then_inc(rl_mm, 1)
            pe.wait_ge(rl_mask, 1)
            ones, tri = cols(C_ONES, P), cols(C_TRI, P)
            pe.matmul(PS[:, 7, 0:8], tri, oh2[:, 0, :], start=True, stop=True)
            pe.matmul(PS[:, 7, 8:16], ones, oh2[:, 0, :], start=True, stop=False)
            pe.matmul(PS[:, 7, 8:16], tri, oh2[:, 1, :], start=False, stop=True)
            pe.matmul(PS[:, 7, 16:24], ones, oh2[:, 0, :], start=True, stop=False)
            pe.matmul(PS[:, 7, 16:24], ones, oh2[:, 1, :], start=False, stop=True).then_inc(rk_mm, 1)
            pe.wait_ge(n_ready, 1)
            turns = pe.value_load(n_sb[0:1, 0:1], min_val=NE, max_val=2 * NE)
            pe.wait_ge(xg_l, 2)
            pe.wait_ge(bank_free, CH_PROJ1)

            def gather(n):
                pe.wait_ge(e_sel, n)
                for kt in range(KT):
                    o = PS[:, 4 + kt // 4, (kt % 4) * P:(kt % 4 + 1) * P]
                    for tt in range(NT):
                        pe.matmul(o, XNH[:, tt, kt * P:(kt + 1) * P], SEL[:, tt, :], start=tt == 0, stop=False)
                        m = pe.matmul(o, XNL[:, tt, kt * P:(kt + 1) * P], SEL[:, tt, :], start=False, stop=tt == 1)
                m.then_inc(e_ga, 1)

            def scatter(tt):
                m = three([[PS[:, 4, :], PS[:, 5, :]]], [(GTH[:, tt * P:(tt + 1) * P], GTL[:, tt * P:(tt + 1) * P])],
                          [(YH[:, c * 512:(c + 1) * 512], YL[:, c * 512:(c + 1) * 512]) for c in range(2)],
                          True, True)
                m.then_inc(e_sc, 1)

            pe.wait_ge(t_low, lows(T_NORM5 - 1))
            gather(1)
            with pe.Fori(0, turns, 1) as it:
                def after_gu(n):
                    if n == 0:
                        pe.wait_ge(e_yl, it + 1)
                        scatter(0)
                    if n == 1:
                        pe.wait_ge(e_add, it * 2 + 1)
                        scatter(1)
                    if n == 4:
                        pe.wait_ge(e_add, it * 2 + 2)
                        pe.wait_ge(e_gsel, it + 1)
                        for tt in range(NT):
                            m = pe.transpose(PS[:, 4, tt * P:(tt + 1) * P], GSEL[:, tt, :], ident)
                        m.then_inc(e_gt, 1)
                    if n == ESTEPS - 1:
                        pe.wait_ge(e_gtl, it + 2)
                        gather(it + 2)

                pe.wait_ge(e_xl, it + 1)
                ffn(ESTEPS, it * ESLABS + A_END, lambda kt: [(XGH[:, kt, :], XGL[:, kt, :])], 1,
                    lambda n, tt: PS[:, 2 + n % 2, :], lambda n: PS[:, 6 + n % 2, :],
                    [[PS[:, 0, :], PS[:, 1, :]]], it * ESTEPS + FSTEPS, after_gu)
            pe.wait_ge(e_xl, turns + 1)
            pe.wait_ge(e_yl, turns + 1)
            scatter(0)
            pe.wait_ge(e_add, turns * 2 + 1)
            scatter(1)
            ple(CH_PROJ1, turns * ESLABS + A_END, A_END, 5, T_NORM5)

        @block.scalar
        def _(act):
            A = nc.scalar.activation
            split = [0]

            def high(count, slot, raw, land, landed, w=SLAB):
                act.wait_ge(land, landed)
                if not isinstance(count, int) or count >= RW:
                    act.wait_ge(slab_used, count + (1 - RW))
                A(WH[:, slot, 0:w], raw[:, 0:w], ACT.Copy).then_inc(high_ready, 1)

            def upto(s):
                while split[0] <= min(s, A_END - 1):
                    i = split[0]
                    high(i, i % RW, RAWA[:, i % RA, :], landA[i % RA], 16 * (i // RA + 1),
                         512 if i == A_P0 else SLAB)
                    split[0] += 1

            def norm(n):
                if n == 0:
                    act.wait_ge(x_in, 16)
                for c in range(2):
                    if n:
                        act.wait_ge(h_ready, 2 * n - 1 + c)
                    for tt in range(NT):
                        A(XN[:, tt, c * 512:(c + 1) * 512], h[:, tt, c * 512:(c + 1) * 512], ACT.Square,
                          accum_out=ss[:, 2 * c + tt:2 * c + tt + 1]).then_inc(sq_done, 1)
                act.wait_ge(ms_done, n + 1)
                A(rt, ms, ACT.Sqrt).then_inc(rt_done, 1)

            def high_t(k, out_of, gains):
                act.wait_ge(t_done, k + 1)
                for i in range(2):
                    m = A(out_of(i), tbank(k)[:, i * S:(i + 1) * S], ACT.Copy, scale=gains(i))
                m.then_inc(t_high, 1)

            def norm_t(n, k0):
                for q in range(4):
                    high_t(k0 + q, lambda i: XTH[:, 2 * q + i, :], lambda i: gain(n, 2 * q + i))

            def copy_t(k, out, src):
                act.wait_ge(t_done, k + 1)
                A(out, src, ACT.Copy).then_inc(t_high, 1)

            def ple(base, c0):
                for c in range(2):
                    if c == 0:
                        act.wait_ge(slab_used, base + 2)
                    for tt in range(NT):
                        m = A(PP[:, tt, c * 512:(c + 1) * 512], pair(c0 + c, tt), ACT.Copy)
                    m.then_inc(bank_free, 1)

            def ple_gate(base, c0, c):
                act.wait_ge(slab_used, base + (4 + 2 * c))
                for tt in range(NT):
                    m = A(PG[:, tt, c * 512:(c + 1) * 512], pair(c0 + 2 + c, tt), ACT.Sigmoid)
                m.then_inc(pg_done, 1)

            norm(0)
            upto(1)
            act.wait_ge(small_in, 16)
            norm_t(0, T_NORM0)
            upto(2)
            act.wait_ge(ang_done, 1)
            A(SIN[:, :, :], SIN[:, :, :], ACT.Sin)
            A(COS[:, :, :], COS[:, :, :], ACT.Sin).then_inc(trig_done, 1)
            A(GRH[:, :, :], W[:, W_GR:W_GR + KT * 32].rearrange("p (k n) -> p k n", k=KT), ACT.Copy).then_inc(gr_high, 1)
            for c in range(12):
                s = A_RIN + 2 * c + 1
                upto(s + 2)
                if 4 <= c < 8:
                    act.wait_ge(slab_used, s + 1)
                    for tt in range(NT):
                        m = A(V[:, tt, (c - 4) * 512:(c - 3) * 512], pair(c, tt), ACT.Copy)
                        m.then_inc(v_done, 1)
                    act.wait_ge(v_done, 2 * (c - 3))
                    if c == 4:
                        act.wait_ge(bank_free, 4)
                    act.sem_inc(bank_free, 1)
                if c >= 8:
                    act.wait_ge(slab_used, s + 1)
                    if c == 8:
                        act.wait_ge(rope_done, 8)
                    for tt in range(NT):
                        A(SG[:, tt, (c - 8) * 512:(c - 7) * 512], pair(c, tt), ACT.Sigmoid).then_inc(sig_done, 1)
                if c >= 4:
                    q = c - 4
                    copy_t(T_QK + q, QKT[:, 2 * q:2 * q + 2, :],
                           tbank(T_QK + q).rearrange("p (k t) -> p k t", k=2))

            def ret_copy(hd):
                act.wait_ge(o_mm, hd + 1)
                if hd == 0:
                    act.wait_ge(t_high, T_Z)
                for tt in range(NT):
                    A(O[:, tt, hd * RDV:(hd + 1) * RDV], pair(CH_O + hd, tt), ACT.Copy).then_inc(o_copied, 1)
                act.wait_ge(o_copied, 2 * (hd + 1))
                if hd == 0:
                    act.wait_ge(bank_free, CH_O)
                act.sem_inc(bank_free, 1)

            def ret_scale(hd):
                act.wait_ge(var_done, hd + 1)
                A(vs_, vr, ACT.Sqrt).then_inc(std_done, 1)
                act.wait_ge(z_done, hd + 1)
                for tt in range(NT):
                    A(O[:, tt, hd * RDV:(hd + 1) * RDV], O[:, tt, hd * RDV:(hd + 1) * RDV], ACT.Copy,
                      scale=vq[:, tt:tt + 1]).then_inc(zs_done, 1)

            def ret_high(hd):
                for j in range(2):
                    f = 4 * hd + 2 * j
                    high_t(T_Z + 2 * hd + j, lambda i: ZTH[:, f + i, :], lambda i: W[:, 48 + f + i:49 + f + i])

            for hd in range(RH):
                ret_copy(hd)
                ret_scale(hd)
                if hd:
                    ret_high(hd - 1)
            ret_high(RH - 1)
            upto(A_FFN + 1)
            norm(1)
            norm_t(1, T_NORM1)

            def f_sigmoid(n, used, tiles, gu_bank, fbase):
                act.wait_ge(slab_used, used)
                if n:
                    act.wait_ge(f_hid, fbase + n)
                for tt in range(tiles):
                    m = A(SIG[:, tt, :], gu_bank(n, tt)[:, 0:256], ACT.Sigmoid)
                m.then_inc(f_sig, 1)

            def f_t_high(n, tiles, t_bank, fbase):
                act.wait_ge(f_t, fbase + (n + 1))
                w = 2 * tiles * P
                A(AT[:, (n % 2) * 2 * w:(n % 2) * 2 * w + w], t_bank(n)[:, 0:w], ACT.Copy).then_inc(f_high, 1)

            for n in range(FSTEPS):
                s = A_FFN + gu_slab(n) + 1
                upto(s + 2)
                f_sigmoid(n, s + 1, NT, lambda n, tt: PS[:, 6 + tt, :], 0)
                upto(s + 3)
                f_t_high(n, NT, lambda n: PS[:, 4 + n % 2, :], 0)
            upto(A_P0 + 1)
            norm(2)
            ple(A_P0, CH_PROJ0)
            norm_t(2, T_NORM2)
            for c in range(2):
                upto(A_P0 + 5 + 2 * c)
                ple_gate(A_P0, CH_PROJ0, c)
            norm(3)
            norm_t(3, T_NORM3)

            for c in range(5):
                s = A_NIN + 2 * c + 1
                upto(s + 2)
                act.wait_ge(slab_used, s + 1)
                for tt in range(NT):
                    b = pair(CH_NIN + c, tt)
                    bb = b.rearrange("p (h d) -> p h d", d=DH)
                    if c == 0:
                        m = A(KVN[:, tt, :, :], bb, ACT.Copy)
                    elif c in (1, 2):
                        hs = 4 * (c - 1)
                        A(Q12[:, tt, hs:hs + 4, :], bb, ACT.Copy)
                        m = A(NC1[:, tt, hs:hs + 4, :], bb, ACT.Square)
                    else:
                        hs = 8 + 2 * (c - 3)
                        A(Q12[:, tt, hs:hs + 2, :], bb[:, 0:2, :], ACT.Copy)
                        A(NC1[:, tt, hs:hs + 2, :], bb[:, 0:2, :], ACT.Square)
                        m = A(VN[:, tt, 2 * (c - 3):2 * (c - 3) + 2, :], bb[:, 2:4, :], ACT.Copy)
                    m.then_inc(n_copied, 1)
                act.wait_ge(n_copied, 2 * (c + 1))
                act.sem_inc(bank_free, 1)
                if c == 1:
                    for q in range(2):
                        copy_t(T_KV + q, KVT[:, 2 * q:2 * q + 2, :],
                               tbank(T_KV + q).rearrange("p (k t) -> p k t", k=2))
                if c in (2, 3):
                    act.wait_ge(tb_raw, c - 1)
                    A(TBH[c - 2], TBR, ACT.Copy).then_inc(tb_high, 1)
                if c >= 3:
                    h0, h1 = (0, 8) if c == 3 else (8, 12)
                    act.wait_ge(n_ms, c - 2)
                    A(rsq.rearrange("p (t h) -> p t h", t=NT)[:, :, h0:h1],
                      msq.rearrange("p (t h) -> p t h", t=NT)[:, :, h0:h1], ACT.Sqrt).then_inc(n_rt, 1)
            act.wait_ge(gate_mm, 1)
            A(gates, PS[:, 6, 0:64].rearrange("p (t n) -> p t n", t=NT)[:, :, 0:24], ACT.Sigmoid).then_inc(gate_sig, 1)
            nb = NG * NCB
            for kv in range(2):
                s = A_CMP + 4 * kv
                upto(s + 5)
                act.wait_ge(slab_used, s + 4)
                x_ = pair(CH_CMP + kv, 0)[0:nb, 0:256]
                if kv:
                    act.wait_ge(g_hid, kv)
                A(GEL[0:nb, 0, :], x_, ACT.Square).then_inc(g_sq, 1)
                act.wait_ge(g_in, kv + 1)
                A(GEL[0:nb, 1, :], GEL[0:nb, 0, :], ACT.Sigmoid, scale=2 * 0.7978845608028654).then_inc(g_sg, 1)
            copy_t(T_HID, HT[:, :, 0:nb], tbank(T_HID)[:, 0:128].rearrange("p (b c) -> p b c", b=4)[:, :, 0:nb])
            act.wait_ge(c2_mm, 1)
            A(CV[0:NCB, :, :], PS[0:NCB, 7, :].rearrange("p (b d) -> p b d", b=4), ACT.Copy).then_inc(c2_cp, 1)
            A(CSQ[0:NCB, 0:2, :], PS[0:NCB, 7, 0:256].rearrange("p (b d) -> p b d", b=2), ACT.Square).then_inc(kc_sq, 1)
            act.wait_ge(kc_ms, 1)
            A(csm[0:NCB, 0:2], cmx[0:NCB, 0:2], ACT.Sqrt).then_inc(kc_rt, 1)
            for q in range(6):
                copy_t(T_Q12 + q, QT[:, 2 * q:2 * q + 2, :], tbank(T_Q12 + q).rearrange("p (k t) -> p k t", k=2))
            copy_t(T_KC, KCT[:, :, 0:NCB], tbank(T_KC)[:, 0:32].rearrange("p (g c) -> p g c", g=2)[:, :, 0:NCB])
            act.wait_ge(cs_sub, 1)
            A(CSC[:, :, 0:NCB], CSC[:, :, 0:NCB], ACT.Exp).then_inc(cs_exp, 1)
            for q in range(4):
                copy_t(T_PC + q, PCT[0:NCB, 2 * q:2 * q + 2, :],
                       tbank(T_PC + q)[0:NCB, :].rearrange("p (k t) -> p k t", k=2))

            def att_exp(m_):
                act.wait_ge(as_msk, m_ + 1)
                b = m_ % 2
                A(ST[:, b, 0:P], ST[:, b, 0:P], ACT.Exp, bias=nmx[:, b, 0:1], accum_out=sme[:, b, 0:1])
                A(ST[:, b, P:3 * P], ST[:, b, P:3 * P], ACT.Exp, bias=nmx[:, b, 1:2],
                  accum_out=sme[:, b, 1:2]).then_inc(as_exp, 1)

            for i in range(2 * NH + 2):
                if i < 2 * NH:
                    att_exp(i)
                if 1 <= i <= 2 * NH:
                    k = T_P + i - 1
                    if i >= 3:
                        act.wait_ge(av_mm, i - 2)
                    copy_t(k, PT[:, (i - 1) % 2, :], tbank(k)[:, 0:384])
                if i >= 2 and i % 2 == 1:
                    hd = (i - 3) // 2
                    act.wait_ge(av_mm, 2 * hd + 2)
                    A(XTH[:, hd, :], pair(CH_NO + hd, 0)[:, 0:S], ACT.Copy).then_inc(oh_done, 1)
            upto(A_END - 1)
            norm(4)
            norm_t(4, T_NORM4)
            act.wait_ge(rl_d, 1)
            A(e2, dif, ACT.Exp).then_inc(rl_e, 1)
            for tt in range(NT):
                act.wait_ge(xg_f, tt + 1)
                A(XNH[:, tt, :], XN[:, tt, :], ACT.Copy).then_inc(xg_h, 1)
            act.wait_ge(n_ready, 1)
            turns = act.value_load(n_sb[0:1, 0:1], min_val=NE, max_val=2 * NE)

            def x_high(n):
                act.wait_ge(e_ga, n)
                for c in range(2):
                    m = A(XGH[:, 4 * c:4 * c + 4, :], PS[:, 4 + c, :].rearrange("p (k t) -> p k t", k=4), ACT.Copy)
                m.then_inc(e_xh, 1)

            def y_high(before):
                act.wait_ge(slab_used, before * ESLABS + A_END)
                for c in range(2):
                    m = A(YH[:, c * 512:(c + 1) * 512], PS[:, c, :], ACT.Copy)
                m.then_inc(e_yh, 1)

            x_high(1)
            with act.Fori(0, turns, 1) as it:
                nxt = [0]

                def ahead(s):
                    while nxt[0] <= min(s, ESLABS - 1):
                        j = nxt[0]
                        high(it * ESLABS + (A_END + j), j % RW, BIG[:, (j % RB) * SLAB:(j % RB + 1) * SLAB],
                             landB[j % RB], it * (16 * ESLABS // RB) + 16 * (j // RB + 1))
                        nxt[0] += 1

                ahead(1)
                y_high(it)
                for n in range(ESTEPS):
                    s = gu_slab(n) + 1
                    ahead(s + LEAD1)
                    f_sigmoid(n, it * ESLABS + (A_END + s + 1), 1, lambda n, tt: PS[:, 2 + n % 2, :],
                              it * ESTEPS + FSTEPS)
                    ahead(s + LEAD2)
                    f_t_high(n, 1, lambda n: PS[:, 6 + n % 2, :], it * ESTEPS + FSTEPS)
                    if n == 4:
                        act.wait_ge(e_gt, it + 1)
                        A(GTH, PS[:, 4, 0:S], ACT.Copy).then_inc(e_gth, 1)
                    if n == ESTEPS - 2:
                        ahead(s + 5)
                        x_high(it + 2)
            y_high(turns)
            base = turns * ESLABS + A_END

            def tail(i):
                high(base + i, i % RW, RAWA[:, i % RA, :], landA[i % RA], 16 * ((A_END + i) // RA + 1),
                     512 if i == 0 else SLAB)

            tail(0)
            tail(1)
            tail(2)
            norm(5)
            ple(base, CH_PROJ1)
            norm_t(5, T_NORM5)
            tail(3)
            tail(4)
            ple_gate(base, CH_PROJ1, 0)
            tail(5)
            ple_gate(base, CH_PROJ1, 1)

        @block.vector
        def _(dve):
            V_ = nc.vector
            steps_ = [0]
            split = [0]

            def link(ins):
                steps_[0] += 1
                ins.then_inc(dve_step, 1)
                dve.wait_ge(dve_step, steps_[0])

            def low(count, slot, raw, w=SLAB):
                dve.wait_ge(high_ready, count + 1)
                V_.tensor_tensor(WL[:, slot, 0:w], raw[:, 0:w], WH[:, slot, 0:w].bitcast(F32),
                                 ALU.subtract).then_inc(low_ready, 1)

            def upto(s):
                while split[0] <= min(s, A_END - 1):
                    i = split[0]
                    low(i, i % RW, RAWA[:, i % RA, :], 512 if i == A_P0 else SLAB)
                    split[0] += 1

            def norm(n, hcount=None):
                dve.wait_ge(sq_done, 4 * (n + 1))
                link(V_.tensor_tensor(ms, ss[:, 0:2], ss[:, 2:4], ALU.add))
                V_.tensor_scalar(ms, ms, 1.0 / D, EPS, ALU.mult, ALU.add).then_inc(ms_done, 1)
                dve.wait_ge(rt_done, n + 1)
                link(V_.reciprocal(rstd, rt))
                for tt in range(NT):
                    V_.tensor_scalar(XN[:, tt, :], h[:, tt, :], rstd[:, tt:tt + 1], None,
                                     ALU.mult).then_inc(xn_done, 1)

            def low_t(k, hi_of, out_of, gains):
                dve.wait_ge(t_high, k + 1)
                for i in range(2):
                    m = V_.scalar_tensor_tensor(out=out_of(i), in0=tbank(k)[:, i * S:(i + 1) * S], scalar=gains(i),
                                                in1=hi_of(i).bitcast(F32), op0=ALU.mult, op1=ALU.subtract)
                m.then_inc(t_low, 1)

            def norm_t(n, k0):
                for q in range(4):
                    low_t(k0 + q, lambda i: XTH[:, 2 * q + i, :], lambda i: XTL[:, 2 * q + i, :],
                          lambda i: gain(n, 2 * q + i))

            def add_to_h(c, tt, nc_):
                hh = h[:, tt, nc_ * 512:(nc_ + 1) * 512]
                return V_.tensor_tensor(hh, hh, pair(c, tt), ALU.add)

            def rope(x_, cs, sn, tc, ts, o, half):
                V_.tensor_tensor(tc, x_, cs, ALU.mult)
                link(V_.tensor_tensor(ts, x_, sn, ALU.mult))
                V_.tensor_tensor(o[:, :, 0, :], tc[:, :, 0, :], ts[:, :, 1, :], ALU.subtract)
                return V_.tensor_tensor(o[:, :, 1, :], tc[:, :, 1, :], ts[:, :, 0, :], ALU.add)

            norm(0)
            upto(1)
            dve.wait_ge(small_in, 16)
            norm_t(0, T_NORM0)
            upto(2)
            dve.wait_ge(pos_in, 16)
            dve.wait_ge(const_in, 16)
            link(V_.tensor_copy(posf, posi[:, 0:3]))
            c1 = 6.28125
            c2 = float(np.float32(TWO_PI - c1))
            c2 = float(np.frombuffer(np.uint32(np.frombuffer(np.float32(c2).tobytes(), np.uint32)[0] & 0xFFFFF000)
                                     .tobytes(), np.float32)[0])
            c3 = float(np.float32(TWO_PI - c1 - c2))
            ang = [TC[:, 0:384].rearrange("p (a n) -> p a n", a=3), TS[:, 0:384].rearrange("p (a n) -> p a n", a=3)]
            magic = float(1.5 * 2 ** 23)
            for a in range(3):
                m = V_.tensor_scalar(ang[0][:, a, :], cols(C_INV, P), posf[:, a:a + 1], None, ALU.mult)
            link(m)
            for dst, quarter in ((SIN, 0.0), (COS, 0.25)):
                k_ = ang[1]
                link(V_.tensor_scalar(k_, ang[0], float(1 / TWO_PI), quarter, ALU.mult, ALU.add))
                link(V_.tensor_scalar(k_, k_, magic, None, ALU.add))
                link(V_.tensor_scalar(k_, k_, magic, None, ALU.subtract))
                link(V_.scalar_tensor_tensor(out=dst[:, :, :], in0=k_, scalar=-c1, in1=ang[0], op0=ALU.mult, op1=ALU.add))
                link(V_.scalar_tensor_tensor(out=dst[:, :, :], in0=k_, scalar=-c2, in1=dst[:, :, :], op0=ALU.mult, op1=ALU.add))
                link(V_.scalar_tensor_tensor(out=dst[:, :, :], in0=k_, scalar=-c3, in1=dst[:, :, :], op0=ALU.mult, op1=ALU.add))
                if quarter:
                    link(V_.tensor_scalar(dst[:, :, :], dst[:, :, :], float(np.pi / 2), None, ALU.add))
                link(V_.tensor_scalar(dst[:, :, :], dst[:, :, :], 3.1415925, -3.1415925, ALU.min, ALU.max))
            dve.sem_inc(ang_done, 1)
            dve.wait_ge(gr_high, 1)
            V_.tensor_tensor(GRL[:, :, :], W[:, W_GR:W_GR + KT * 32].rearrange("p (k n) -> p k n", k=KT),
                             GRH[:, :, :].bitcast(F32), ALU.subtract).then_inc(gr_low, 1)
            V_.memset(RT[:, 4096 + 3840:8192].bitcast(F32), 0.0)
            dve.wait_ge(trig_done, 1)
            for c in range(12):
                s = A_RIN + 2 * c + 1
                upto(s + 2)
                if c < 4:
                    dve.wait_ge(slab_used, s + 1)
                    for tt in range(NT):
                        v4 = lambda a: a.rearrange("p (h f d) -> p h f d", h=2, f=2)
                        bc = lambda t: t[:, tt, :].unsqueeze(1).unsqueeze(1).to_broadcast([P, 2, 2, P])
                        m = rope(v4(pair(c, tt)), bc(COS), bc(SIN), v4(TC), v4(TS),
                                 v4(O[:, tt, c * 512:(c + 1) * 512]), P)
                        m.then_inc(rope_done, 1)
                        dve.wait_ge(rope_done, 2 * c + tt + 1)
                    dve.sem_inc(bank_free, 1)
                if c >= 8:
                    for tt in range(NT):
                        dve.wait_ge(sig_done, 2 * (c - 8) + tt + 1)
                        g_ = SG[:, tt, (c - 8) * 512:(c - 7) * 512]
                        V_.tensor_tensor(g_, g_, pair(c, tt), ALU.mult).then_inc(sg_done, 1)
                    dve.wait_ge(sg_done, 2 * (c - 7))
                    if c == 8:
                        dve.wait_ge(bank_free, 8)
                    dve.sem_inc(bank_free, 1)

            def ret_mask(hd):
                dve.wait_ge(sc_done, hd + 1)
                if hd >= 2:
                    dve.wait_ge(o_mm, hd - 1)
                b = PS[:, 6 + hd % 2, :]
                dec = C_DEC + hd * 256
                V_.tensor_tensor(ST[:, hd % 2, 0:S], b[:, 0:S], cols(dec, S), ALU.mult)
                V_.tensor_tensor(ST[:, hd % 2, S:S + P], b[:, S:S + P], cols(dec, P), ALU.mult).then_inc(st_done, 1)

            def ret_norm(hd):
                sl = slice(hd * RDV, (hd + 1) * RDV)
                dve.wait_ge(o_copied, 2 * (hd + 1))
                for tt in range(NT):
                    m = V_.bn_stats(bst[:, tt, :], O[:, tt, sl])
                link(m)
                for tt in range(NT):
                    m = V_.bn_aggr(mv[:, tt, :], bst[:, tt, :])
                link(m)
                V_.tensor_scalar(vr, mv[:, :, 1], EPS, None, ALU.add).then_inc(var_done, 1)
                if hd >= 1:
                    dve.wait_ge(zs_done, 2 * hd)
                dve.wait_ge(std_done, hd + 1)
                V_.reciprocal(vq, vs_)
                for tt in range(NT):
                    m = V_.scalar_tensor_tensor(out=O[:, tt, sl], in0=O[:, tt, sl], scalar=mv[:, tt, 0:1],
                                                in1=SG[:, tt, sl], op0=ALU.subtract, op1=ALU.mult)
                m.then_inc(z_done, 1)

            def ret_low(hd):
                for j in range(2):
                    f = 4 * hd + 2 * j
                    low_t(T_Z + 2 * hd + j, lambda i: ZTH[:, f + i, :], lambda i: ZTL[:, f + i, :],
                          lambda i: W[:, 48 + f + i:49 + f + i])

            ret_mask(0)
            for hd in range(RH):
                if hd + 1 < RH:
                    ret_mask(hd + 1)
                ret_norm(hd)
                if hd:
                    ret_low(hd - 1)
            ret_low(RH - 1)
            for c in range(2):
                s = A_ROUT + 4 * c + 3
                upto(s + 2)
                dve.wait_ge(slab_used, s + 1)
                for tt in range(NT):
                    m = add_to_h(CH_ROUT + c, tt, c)
                link(m)
                if c == 0:
                    dve.wait_ge(bank_free, CH_ROUT)
                dve.sem_inc(h_ready, 1)
                dve.sem_inc(bank_free, 1)
            norm(1)
            norm_t(1, T_NORM1)

            def f_hidden(n, fbase, tiles, gu_bank, linked):
                dve.wait_ge(f_sig, fbase + (n + 1))
                for tt in range(tiles):
                    m = V_.tensor_tensor(SIG[:, tt, :], SIG[:, tt, :], gu_bank(n, tt)[:, 0:256], ALU.mult)
                linked(m)
                for tt in range(tiles):
                    m = V_.tensor_tensor(HID[:, tt, :], SIG[:, tt, :], gu_bank(n, tt)[:, 256:512], ALU.mult)
                m.then_inc(f_hid, 1)

            def f_t_low(n, tiles, t_bank, fbase):
                dve.wait_ge(f_high, fbase + (n + 1))
                w = 2 * tiles * P
                a = (n % 2) * 2 * w
                V_.tensor_tensor(AT[:, a + w:a + 2 * w], t_bank(n)[:, 0:w], AT[:, a:a + w].bitcast(F32),
                                 ALU.subtract).then_inc(f_low, 1)

            for n in range(FSTEPS):
                s = A_FFN + gu_slab(n) + 1
                upto(s + 2)
                f_hidden(n, 0, NT, lambda n, tt: PS[:, 6 + tt, :], link)
                upto(s + 3)
                f_t_low(n, NT, lambda n: PS[:, 4 + n % 2, :], 0)
            upto(A_P0 + 1)
            dve.wait_ge(slab_used, A_P0)
            for c in range(2):
                for tt in range(NT):
                    m = add_to_h(CH_FFN + c, tt, c)
                link(m)
                dve.sem_inc(h_ready, 1)
                dve.sem_inc(bank_free, 1)

            def ple_add(c, last=False):
                dve.wait_ge(pg_done, c + 1)
                cc = c % 2
                for tt in range(NT):
                    g_ = PG[:, tt, cc * 512:(cc + 1) * 512]
                    m = V_.tensor_tensor(g_, g_, PP[:, tt, cc * 512:(cc + 1) * 512], ALU.mult)
                link(m)
                for tt in range(NT):
                    hh = h[:, tt, cc * 512:(cc + 1) * 512]
                    m = V_.tensor_tensor(hh, hh, PG[:, tt, cc * 512:(cc + 1) * 512], ALU.add)
                link(m)
                dve.sem_inc(h_ready, 1)
                dve.sem_inc(bank_free, 1)

            norm(2)
            norm_t(2, T_NORM2)
            for c in range(2):
                upto(A_P0 + 5 + 2 * c)
                ple_add(c)
            norm(3)
            norm_t(3, T_NORM3)
            upto(A_NIN + 5)
            dve.wait_ge(t_high, T_KV + 2)
            for kv in range(2):
                if kv:
                    dve.wait_ge(tb_low, kv)
                tb4 = TBR.rearrange("p (l g c) -> p l g c", l=LC, g=NG)
                pe_ = W[:, W_POS + kv * LC:W_POS + (kv + 1) * LC]
                for g in range(NG):
                    src = KVT[:, 2 * kv + g, :]
                    for half in range(2):
                        tok = src[:, 16 * half:16 * half + 16 * NCB].rearrange("p (c l) -> p l c", l=STR)
                        m = V_.tensor_tensor(tb4[:, 16 * half:16 * half + 16, g, :], tok,
                                             pe_[:, 16 * half:16 * half + 16].unsqueeze(2).to_broadcast([P, STR, NCB]),
                                             ALU.add)
                m.then_inc(tb_raw, 1)
                dve.wait_ge(tb_high, kv + 1)
                V_.tensor_tensor(TBL[kv], TBR, TBH[kv].bitcast(F32), ALU.subtract).then_inc(tb_low, 1)
                upto(A_NIN + 7 + 2 * kv)
            sq3, mq3, rq3 = (v.rearrange("p (t h) -> p t h", t=NT) for v in (ssq, msq, riq))

            def norm_rope(h0, h1, i, copied, slab, last):
                dve.wait_ge(n_copied, copied)
                link(V_.tensor_reduce(sq3[:, :, h0:h1], NC1[:, :, h0:h1, :], AXX, ALU.add))
                V_.tensor_scalar(mq3[:, :, h0:h1], sq3[:, :, h0:h1], 1.0 / DH, EPS, ALU.mult, ALU.add).then_inc(n_ms, 1)
                dve.wait_ge(n_rt, i + 1)
                link(V_.reciprocal(rq3[:, :, h0:h1], rsq.rearrange("p (t h) -> p t h", t=NT)[:, :, h0:h1]))
                for tt in range(NT):
                    m = V_.tensor_tensor(Q12[:, tt, h0:h1, :], Q12[:, tt, h0:h1, :],
                                         rq3[:, tt, h0:h1].unsqueeze(2).to_broadcast([P, h1 - h0, DH]), ALU.mult)
                link(m)
                upto(slab)
                for tt in range(NT):
                    for a, b_, g in (((0, 8, 0),) if h0 == 0 else ((8, 10, 2), (10, 12, 3))):
                        m = V_.tensor_tensor(Q12[:, tt, a:b_, :], Q12[:, tt, a:b_, :],
                                             rep(g).unsqueeze(1).to_broadcast([P, b_ - a, DH]), ALU.mult)
                link(m)
                upto(min(slab + 1, last))
                for tt in range(NT):
                    v4 = lambda a: a[:, tt, h0:h1, :].rearrange("p h (f d) -> p h f d", f=2)
                    bc = lambda t: t[:, tt, 0:P:2].unsqueeze(1).unsqueeze(1).to_broadcast([P, h1 - h0, 2, 64])
                    m = rope(v4(Q12), bc(COS), bc(SIN), v4(NC1), v4(NC2), v4(Q12), 64)
                    upto(min(slab + 2 + tt, last))
                link(m)
                dve.sem_inc(n_rope, 1)

            norm_rope(0, 8, 0, 6, A_NIN + 10, A_NIN + 11)
            norm_rope(8, 12, 1, 10, A_NIN + 12, A_NIN + 15)
            nb = NG * NCB
            for kv in range(2):
                upto(A_CMP + 4 * kv + 5)
                x_ = pair(CH_CMP + kv, 0)[0:nb, 0:256]
                dve.wait_ge(g_sq, kv + 1)
                link(V_.tensor_scalar(GEL[0:nb, 0, :], GEL[0:nb, 0, :], 0.044715, 1.0, ALU.mult, ALU.add))
                V_.tensor_tensor(GEL[0:nb, 0, :], GEL[0:nb, 0, :], x_, ALU.mult).then_inc(g_in, 1)
                dve.wait_ge(g_sg, kv + 1)
                link(V_.tensor_tensor(GEL[0:nb, 2 + kv, :], GEL[0:nb, 1, :], x_, ALU.mult))
                if kv == 0:
                    dve.wait_ge(bank_free, CH_CMP)
                dve.sem_inc(g_hid, 1)
                dve.sem_inc(bank_free, 1)
            dve.wait_ge(kc_sq, 1)
            link(V_.tensor_reduce(crc[0:NCB, 0:2], CSQ[0:NCB, 0:2, :], AXX, ALU.add))
            V_.tensor_scalar(cmx[0:NCB, 0:2], crc[0:NCB, 0:2], 1.0 / DH, EPS, ALU.mult, ALU.add).then_inc(kc_ms, 1)
            dve.wait_ge(kc_rt, 1)
            link(V_.reciprocal(crc[0:NCB, 0:2], csm[0:NCB, 0:2]))
            kc = CV[0:NCB, 0:2, :]
            link(V_.tensor_tensor(kc, kc, crc[0:NCB, 0:2].unsqueeze(2).to_broadcast([NCB, 2, DH]), ALU.mult))
            link(V_.tensor_tensor(kc, kc, rep(1)[0:NCB, :].unsqueeze(1).to_broadcast([NCB, 2, DH]), ALU.mult))
            v4 = lambda a: a.rearrange("p h (f d) -> p h f d", f=2)
            bc = lambda t: t[0:NCB, 2, 0:P:2].unsqueeze(1).unsqueeze(1).to_broadcast([NCB, 2, 2, 64])
            tmp = NC1[0:NCB, 1, 8:12, :]
            rope(v4(kc), bc(COS), bc(SIN), v4(tmp[:, 0:2, :]), v4(tmp[:, 2:4, :]), v4(CSQ[0:NCB, 2:4, :]), 64
                 ).then_inc(kc_rope, 1)
            dve.wait_ge(cs_mm, 1)
            scale = DH ** -0.5
            pc = CSC[:, :, 0:NCB]
            for tt in range(NT):
                o = CSC[:, tt * NH:(tt + 1) * NH, 0:NCB]
                m = V_.scalar_tensor_tensor(
                    out=o, in0=PS[:, 6, tt * P:(tt + 1) * P].rearrange("p (h c) -> p h c", h=NH)[:, :, 0:NCB],
                    scalar=scale, in1=cols(C_CADD + tt * NCB, NCB).unsqueeze(1).to_broadcast([P, NH, NCB]),
                    op0=ALU.mult, op1=ALU.add)
            link(m)
            link(V_.tensor_reduce(cmx, pc, AXX, ALU.max))
            V_.tensor_tensor(pc, pc, cmx.unsqueeze(2).to_broadcast([P, 16, NCB]), ALU.subtract).then_inc(cs_sub, 1)
            dve.wait_ge(cs_exp, 1)
            link(V_.tensor_reduce(csm, pc, AXX, ALU.add))
            link(V_.reciprocal(crc, csm))
            dve.wait_ge(gate_sig, 1)
            g3 = gates.rearrange("p t (h b) -> p t h b", b=3)
            link(V_.tensor_tensor(crc.rearrange("p (t h) -> p t h", t=NT), crc.rearrange("p (t h) -> p t h", t=NT),
                                  g3[:, :, :, 0], ALU.mult))
            link(V_.tensor_tensor(pc, pc, crc.unsqueeze(2).to_broadcast([P, 16, NCB]), ALU.mult))
            for tt in range(NT):
                o = CSC[:, tt * NH:(tt + 1) * NH, 0:NCB]
                m = V_.tensor_tensor(o, o, cols(C_C01 + tt * NCB, NCB).unsqueeze(1).to_broadcast([P, NH, NCB]), ALU.mult)
            m.then_inc(cp_done, 1)

            def att_mask(m_):
                b = m_ % 2
                dve.wait_ge(as_mm, m_ + 1)
                if m_ >= 2:
                    dve.wait_ge(t_done, T_P + m_ - 1)
                link(V_.scalar_tensor_tensor(out=ST[:, b, :], in0=PS[:, 6 + b, 0:384], scalar=scale,
                                             in1=cols(C_M384, 384), op0=ALU.mult, op1=ALU.add))
                V_.tensor_reduce(nmx[:, b, 0:1], ST[:, b, 0:P], AXX, ALU.max, negate=True)
                V_.tensor_reduce(nmx[:, b, 1:2], ST[:, b, P:3 * P], AXX, ALU.max, negate=True).then_inc(as_msk, 1)

            def att_norm(m_):
                b, hd, br = m_ % 2, m_ // 2, m_ % 2
                dve.wait_ge(as_exp, m_ + 1)
                link(V_.reciprocal(rce[:, b, :], sme[:, b, :]))
                link(V_.tensor_tensor(rce[:, b, :], rce[:, b, :], g3[:, :, hd, 1 + br], ALU.mult))
                V_.tensor_scalar(ST[:, b, 0:P], ST[:, b, 0:P], rce[:, b, 0:1], None, ALU.mult)
                V_.tensor_scalar(ST[:, b, P:3 * P], ST[:, b, P:3 * P], rce[:, b, 1:2], None, ALU.mult).then_inc(ap_done, 1)

            for i in range(2 * NH + 3):
                if i < 2 * NH:
                    att_mask(i)
                if 1 <= i <= 2 * NH:
                    att_norm(i - 1)
                if i >= 4 and i % 2 == 0:
                    hd = (i - 4) // 2
                    dve.wait_ge(oh_done, hd + 1)
                    link(V_.tensor_tensor(XTL[:, hd, :], pair(CH_NO + hd, 0)[:, 0:S],
                                          XTH[:, hd, :].bitcast(F32), ALU.subtract))
                    dve.sem_inc(ol_done, 1)
                    dve.sem_inc(bank_free, 1)
            for c in range(2):
                s = A_NOUT + 2 * c + 1
                upto(s + 2)
                dve.wait_ge(slab_used, s + 1)
                for tt in range(NT):
                    m = add_to_h(CH_NOUT + c, tt, c)
                link(m)
                dve.sem_inc(h_ready, 1)
                dve.sem_inc(bank_free, 1)
            norm(4)
            norm_t(4, T_NORM4)
            dve.wait_ge(grep_ld, 16)
            for tt in range(NT):
                V_.tensor_tensor(XN[:, tt, :], XN[:, tt, :], GREP, ALU.mult).then_inc(xg_f, 1)
            dve.wait_ge(rl_mm, 1)
            link(V_.tensor_copy(lg, PS[:, 6, 0:64].rearrange("p (t n) -> p t n", t=NT)[:, :, 0:8]))
            for tt in range(NT):
                m = V_.max(mx8[:, tt, :], lg[:, tt, :])
            link(m)
            for tt in range(NT):
                m = V_.max_index(idx[:, tt, :], mx8[:, tt, :], lg[:, tt, :])
            link(m)
            link(V_.tensor_copy(ixf, idx[:, :, :]))
            V_.tensor_tensor(dif, mx8[:, :, 1], mx8[:, :, 0], ALU.subtract).then_inc(rl_d, 1)
            for tt in range(NT):
                V_.tensor_scalar(oh1[:, tt, :], cols(C_I8, 8), ixf[:, tt, 0:1], None, ALU.is_equal)
                m = V_.tensor_scalar(oh2[:, tt, :], cols(C_I8, 8), ixf[:, tt, 1:2], None, ALU.is_equal)
            link(m)
            dve.wait_ge(rl_e, 1)
            link(V_.tensor_scalar(den, e2, 1.0, None, ALU.add))
            link(V_.reciprocal(w1, den))
            link(V_.tensor_tensor(w2, e2, w1, ALU.mult))
            for tt in range(NT):
                m = V_.tensor_scalar(GT2[:, tt, 0:8], oh1[:, tt, :], w1[:, tt:tt + 1], None, ALU.mult)
            link(m)
            for tt in range(NT):
                m = V_.scalar_tensor_tensor(out=GT2[:, tt, 0:8], in0=oh2[:, tt, :], scalar=w2[:, tt:tt + 1],
                                            in1=GT2[:, tt, 0:8], op0=ALU.mult, op1=ALU.add)
            link(m)
            V_.tensor_copy(GT2[:, :, 8:16], GT2[:, :, 0:8])
            V_.tensor_tensor(oh2, oh2, oh1, ALU.add).then_inc(rl_mask, 1)
            dve.wait_ge(rl_mask, 1)
            link(V_.tensor_scalar(oh1, oh2, -10000.0, 10000.0, ALU.mult, ALU.add))
            dve.wait_ge(rk_mm, 1)
            link(V_.tensor_tensor(RK[:, :, 0:8], oh1, PS[:, 7, 0:16].rearrange("p (t n) -> p t n", t=NT), ALU.add))
            V_.tensor_scalar(RK[:, :, 8:16], RK[:, :, 0:8], -float(P), None, ALU.add)
            V_.memset(RK[:, :, 16:17], -1.0)
            link(V_.tensor_reduce(mxc, PS[:, 7, 16:24], AXX, ALU.max))
            V_.tensor_scalar(nfl[:, 0:1], mxc, float(P), float(NE), ALU.is_gt, ALU.mult)
            link(V_.tensor_scalar(nfl[:, 1:2], mxc, float(P), None, ALU.is_gt))
            V_.tensor_scalar(n_sb[:, 0:1], nfl[:, 0:1], float(NE), None, ALU.add)
            V_.tensor_scalar(n_sb[:, 1:2], nfl[:, 1:2], 1.0, None, ALU.add).then_inc(n_ready, 1)
            for tt in range(NT):
                dve.wait_ge(xg_h, tt + 1)
                V_.tensor_tensor(XNL[:, tt, :], XN[:, tt, :], XNH[:, tt, :].bitcast(F32),
                                 ALU.subtract).then_inc(xg_l, 1)
            dve.wait_ge(xg_l, 2)
            dve.wait_ge(n_ready, 1)
            turns = dve.value_load(n_sb[0:1, 0:1], min_val=NE, max_val=2 * NE)

            def select(i):
                for tt in range(NT):
                    m = V_.tensor_scalar(SEL[:, tt, :], cols(C_IOTA, P), RK[:, tt, bass.ds(i, 1)], None, ALU.is_equal)
                m.then_inc(e_sel, 1)

            def x_low(n):
                dve.wait_ge(e_xh, n)
                for c in range(2):
                    m = V_.tensor_tensor(XGL[:, 4 * c:4 * c + 4, :], PS[:, 4 + c, :].rearrange("p (k t) -> p k t", k=4),
                                         XGH[:, 4 * c:4 * c + 4, :].bitcast(F32), ALU.subtract)
                m.then_inc(e_xl, 1)

            def y_low(n):
                dve.wait_ge(e_yh, n)
                for c in range(2):
                    m = V_.tensor_tensor(YL[:, c * 512:(c + 1) * 512], PS[:, c, :],
                                         YH[:, c * 512:(c + 1) * 512].bitcast(F32), ALU.subtract)
                m.then_inc(e_yl, 1)

            def expert_add(tt, n):
                dve.wait_ge(e_sc, n)
                for c in range(2):
                    hh = h[:, tt, c * 512:(c + 1) * 512]
                    m = V_.tensor_tensor(hh, hh, PS[:, 4 + c, :], ALU.add)
                m.then_inc(e_add, 1)

            V_.memset(GTH.bitcast(F32), 0.0)
            V_.memset(GTL.bitcast(F32), 0.0).then_inc(e_gtl, 1)
            select(0)
            x_low(1)
            with dve.Fori(0, turns, 1) as it:
                nxt = [0]

                def ahead(s):
                    while nxt[0] <= min(s, ESLABS - 1):
                        j = nxt[0]
                        low(it * ESLABS + (A_END + j), j % RW, BIG[:, (j % RB) * SLAB:(j % RB + 1) * SLAB])
                        nxt[0] += 1

                lk = [0]

                def elink(m):
                    lk[0] += 1
                    m.then_inc(hid_step, 1)
                    dve.wait_ge(hid_step, it * ESTEPS + lk[0])

                ahead(1)
                y_low(it + 1)
                for n in range(ESTEPS):
                    s = gu_slab(n) + 1
                    ahead(s + LEAD1)
                    f_hidden(n, it * ESTEPS + FSTEPS, 1, lambda n, tt: PS[:, 2 + n % 2, :], elink)
                    ahead(s + LEAD2)
                    f_t_low(n, 1, lambda n: PS[:, 6 + n % 2, :], it * ESTEPS + FSTEPS)
                    if n < NT:
                        expert_add(n, it * 2 + (n + 1))
                    if n == 2:
                        for tt in range(NT):
                            m = V_.tensor_scalar(GSEL[:, tt, :], cols(C_IOTA, P), RK[:, tt, bass.ds(it, 1)],
                                                 GT2[:, tt, bass.ds(it, 1)], ALU.is_equal, ALU.mult)
                        m.then_inc(e_gsel, 1)
                    if n == 4:
                        dve.wait_ge(e_gth, it + 1)
                        V_.tensor_tensor(GTL, PS[:, 4, 0:S], GTH.bitcast(F32), ALU.subtract).then_inc(e_gtl, 1)
                    if n == 8:
                        select(it + 1)
                    if n == ESTEPS - 2:
                        ahead(s + 5)
                        x_low(it + 2)
            y_low(turns + 1)
            for tt in range(NT):
                expert_add(tt, turns * 2 + (tt + 1))
            dve.wait_ge(e_add, turns * 2 + 2)
            dve.sem_inc(h_ready, 2)
            base = turns * ESLABS + A_END

            def tail(i):
                low(base + i, i % RW, RAWA[:, i % RA, :], 512 if i == 0 else SLAB)

            tail(0)
            tail(1)
            tail(2)
            norm(5)
            norm_t(5, T_NORM5)
            tail(3)
            tail(4)
            ple_add(2)
            tail(5)
            ple_add(3)


def slabs_k(w):
    k, n = w.shape
    return w.reshape(k // 512, 4, P, n // 512, 512).transpose(3, 0, 2, 1, 4).reshape(-1, P, SLAB)


def slabs_r(w, kt):
    k, n = w.shape
    return w.reshape(k // (kt * P), kt, P, n).transpose(0, 2, 1, 3).reshape(-1, P, kt * n)


def slabs_ffn(gu, down):
    f = down.shape[0]
    steps = f // 256
    both = np.concatenate([gu[:, :f].reshape(D, steps, 256), gu[:, f:].reshape(D, steps, 256)], axis=2)
    g = slabs_k(both.reshape(D, steps * 512))
    d = slabs_r(down, 2)
    order = [g[0], g[1]]
    for n in range(1, steps):
        order += [g[2 * n], g[2 * n + 1], d[n - 1]]
    order.append(d[steps - 1])
    return np.stack(order)


def p_slab(p):
    s = np.zeros((1, P, SLAB), np.float32)
    s[0, :, 0:512] = p.T.reshape(2, P, S).transpose(1, 0, 2).reshape(P, 512)
    return s


def kernel(x, p, positions, norm_mix, norm_ffn, norm_ple,
           ret_w_in, ret_gn, ret_w_out,
           nsa_w_in, nsa_q_norm, nsa_k_norm, nsa_cmp_pos, nsa_cmp_w1, nsa_cmp_w2, nsa_w_out,
           s5_w_in, s5_a_re, s5_a_im, s5_b_re, s5_b_im, s5_c_re, s5_c_im, s5_d, s5_log_dt, s5_w_glu,
           ffn_w_gate_up, ffn_w_down,
           moe_router, moe_w_gate_up, moe_w_down,
           ple_w_proj, ple_w_gate):
    import concourse.bacc as bacc
    from concourse.bass_utils import run_bass_kernel_spmd

    a = lambda v: np.asarray(v)
    x, p, positions = a(x), a(p), a(positions)
    nin = a(nsa_w_in)[0]
    kvw = NG * DH
    nin_main = np.concatenate([nin[:, D:D + 2 * kvw], nin[:, 0:D], nin[:, D + 2 * kvw:D + 6 * kvw]], axis=1)
    w1 = a(nsa_cmp_w1)[0]
    static = np.concatenate([
        slabs_k(a(ret_w_in)[0]), slabs_k(a(ret_w_out)[0]), slabs_ffn(a(ffn_w_gate_up)[0], a(ffn_w_down)[0]),
        p_slab(p[0, 0]), slabs_r(a(ple_w_proj)[0], 2), slabs_k(a(ple_w_gate)[0]),
        slabs_k(nin_main), slabs_r(w1[0], 8), slabs_r(w1[1], 8), slabs_k(a(nsa_w_out)[0]),
        p_slab(p[1, 0]), slabs_r(a(ple_w_proj)[1], 2), slabs_k(a(ple_w_gate)[1])])
    gu, dn = a(moe_w_gate_up)[0], a(moe_w_down)[0]
    expert = np.stack([slabs_ffn(gu[e], dn[e]) for e in range(NE)])

    small = np.zeros((P, W_END), np.float32)
    nm, nf, npl = a(norm_mix), a(norm_ffn), a(norm_ple)
    for i, g in enumerate((nm[0], nf[0], npl[0], nm[1], nf[1], npl[1])):
        small[:, i * KT:(i + 1) * KT] = g.reshape(KT, P).T
    small[:, 48:64] = a(ret_gn)[0].reshape(16, P).T
    kn = a(nsa_k_norm)[0]
    for i, g in enumerate((a(nsa_q_norm)[0], kn[0], kn[1], kn[2])):
        small[:, W_REP + i * DH:W_REP + (i + 1) * DH] = np.broadcast_to(g, (P, DH))
    small[:, W_POS:W_POS + 2 * LC] = a(nsa_cmp_pos)[0].transpose(2, 0, 1).reshape(P, 2 * LC)
    small[:, W_W2:W_GR] = a(nsa_cmp_w2)[0].reshape(2, 2, P, DH).transpose(2, 0, 1, 3).reshape(P, 4 * DH)
    gr = np.concatenate([nin[:, D + 6 * kvw:], a(moe_router)[0]], axis=1)
    small[:, W_GR:] = gr.reshape(KT, P, 32).transpose(1, 0, 2).reshape(P, KT * 32)
    pos = np.zeros((P, 4), np.int32)
    pos[:, 0:NT] = positions[0].reshape(NT, P).T
    pos[0:NCB, 2] = positions[0, 0:STR * NCB:STR]
    arrays = {
        "x_dram": np.ascontiguousarray(x[0]), "pos_dram": pos, "const_dram": const_array(), "small_dram": small,
        "gain_dram": np.ascontiguousarray(np.broadcast_to(nf[1], (P, D))),
        "static_dram": static, "expert_dram": expert,
    }
    nc = bacc.Bacc("TRN2", target_bir_lowering=False, num_devices=1)
    args = [nc.dram_tensor(n, v.shape, mybir.dt.from_np(v.dtype), kind="ExternalInput").ap() for n, v in arrays.items()]
    out = nc.dram_tensor("out_dram", (S, D), F32, kind="ExternalOutput").ap()
    build(nc, *args, out)
    r = run_bass_kernel_spmd(nc, [arrays], core_ids=[0])
    return np.asarray(r.results[0]["out_dram"]).reshape(1, S, D)
```
